# Optimizing a Trainium2 kernel written in Bass

```python
import jax, jax.numpy as jnp
from jax import lax
import numpy as np

D_MODEL = 1024
BATCH = 1
SEQ = 512
DEPTH = 2

CTX_LEN = 256
GRID_W = 64
EPS = 1e-6

FOURIER_GROUPS = 4
FOURIER_GD = 64
FOURIER_W = FOURIER_GROUPS * FOURIER_GD
ATT_HEADS = 8
ATT_KV_HEADS = 2
ATT_GROUP = ATT_HEADS // ATT_KV_HEADS
HEAD_DIM = 64
ATT_W = ATT_HEADS * HEAD_DIM
ATT_KV_W = ATT_KV_HEADS * HEAD_DIM
HG_HEADS = 4
HG_DK = 64
HG_DV = 64
HG_W = HG_HEADS * HG_DK
MIX_W = FOURIER_W + ATT_W + HG_W

OFF_FOURIER = 0
OFF_Q = OFF_FOURIER + FOURIER_W
OFF_K = OFF_Q + ATT_W
OFF_V = OFF_K + ATT_KV_W
OFF_FF = OFF_V + ATT_KV_W
OFF_FB = OFF_FF + HG_W
OFF_I = OFF_FB + HG_W
OFF_HQ = OFF_I + HG_W
OFF_G = OFF_HQ + HG_W
PROJ_W = OFF_G + HG_W

D_FF = -(-8 * D_MODEL // (3 * 256)) * 256
ROPE_THETA = 10000.0
Q_BLOCK = 128
HG_CHUNK = 64


def rmsnorm(x, gain=None):
    xf = x.astype(jnp.float32)
    y = xf * lax.rsqrt(jnp.mean(xf * xf, axis=-1, keepdims=True) + EPS)
    if gain is not None:
        y = y * gain.astype(jnp.float32)
    return y.astype(x.dtype)

def col(u, off, width, base=0):
    return u[..., off - base: off - base + width]

def axial_rope_tables(n):
    rows = n // GRID_W
    row = jnp.repeat(jnp.arange(rows), GRID_W).astype(jnp.float32)
    colp = jnp.tile(jnp.arange(GRID_W), rows).astype(jnp.float32)
    half = HEAD_DIM // 2
    freqs = ROPE_THETA ** (-jnp.arange(0, half, 2, dtype=jnp.float32) / half)
    ang_r = row[:, None] * freqs
    ang_c = colp[:, None] * freqs
    return (jnp.cos(ang_r), jnp.sin(ang_r), jnp.cos(ang_c), jnp.sin(ang_c))

def rope_axis(x, cos, sin):
    x1, x2 = jnp.split(x, 2, axis=-1)
    return jnp.concatenate([x1 * cos - x2 * sin, x1 * sin + x2 * cos], axis=-1)

def apply_axial_rope(x, tabs):
    cr, sr, cc, sc = tabs
    xf = x.astype(jnp.float32)
    xr, xc = jnp.split(xf, 2, axis=-1)
    return jnp.concatenate([rope_axis(xr, cr, sr), rope_axis(xc, cc, sc)], axis=-1).astype(x.dtype)

def fourier_mix(u, w):
    b, n, _ = u.shape
    z = u.astype(jnp.float32).reshape(b, n, FOURIER_GROUPS, FOURIER_GD)
    z = jnp.fft.fftn(z, axes=(1, 3), norm="ortho").real
    return z.reshape(b, n, FOURIER_W).astype(u.dtype) @ w

def attend(q, k, v):
    s = jnp.einsum('bkgqd,bksd->bkgqs', q, k).astype(jnp.float32) * (HEAD_DIM ** -0.5)
    p = jax.nn.softmax(s, axis=-1).astype(v.dtype)
    return jnp.einsum('bkgqs,bksd->bkgqd', p, v)

def attend_blocked(q, k, v):
    b, kh, g, n, d = q.shape
    nb = n // Q_BLOCK
    qb = jnp.moveaxis(q.reshape(b, kh, g, nb, Q_BLOCK, d), 3, 0)
    ob = lax.map(lambda qi: attend(qi, k, v), qb)
    return jnp.moveaxis(ob, 0, 3).reshape(b, kh, g, n, d)

def q_heads(u, gain):
    b, n, _ = u.shape
    return rmsnorm(u.reshape(b, n, ATT_HEADS, HEAD_DIM), gain).transpose(0, 2, 1, 3)

def kv_heads(u, gain=None):
    b, n, _ = u.shape
    return rmsnorm(u.reshape(b, n, ATT_KV_HEADS, HEAD_DIM), gain).transpose(0, 2, 1, 3) if gain is not None \
        else u.reshape(b, n, ATT_KV_HEADS, HEAD_DIM).transpose(0, 2, 1, 3)

def group_q(qh):
    b, h, n, d = qh.shape
    return qh.reshape(b, ATT_KV_HEADS, ATT_GROUP, n, d)

def ungroup(o):
    b, kh, g, n, d = o.shape
    return o.transpose(0, 3, 1, 2, 4).reshape(b, n, kh * g * d)

def attention_group(ux, uc, base_c, q_gain, k_gain, tabs, ctx_out):
    qx = group_q(apply_axial_rope(q_heads(col(ux, OFF_Q, ATT_W), q_gain), tabs))
    kx = apply_axial_rope(kv_heads(col(ux, OFF_K, ATT_KV_W), k_gain), tabs)
    vx = kv_heads(col(ux, OFF_V, ATT_KV_W))
    kc = kv_heads(col(uc, OFF_K, ATT_KV_W, base_c), k_gain)
    vc = kv_heads(col(uc, OFF_V, ATT_KV_W, base_c))
    k_all = jnp.concatenate([kc, kx], axis=2)
    v_all = jnp.concatenate([vc, vx], axis=2)
    out_x = ungroup(attend_blocked(qx, k_all, v_all))
    out_c = None
    if ctx_out:
        qc = group_q(q_heads(col(uc, OFF_Q, ATT_W, base_c), q_gain))
        out_c = ungroup(attend(qc, kc, vc))
    return out_x, out_c

def hgrn_scan(k, v, log_f, s0, q=None):
    b, h, n, dk = k.shape
    nc = n // HG_CHUNK
    with_out = q is not None

    def chunks(a):
        return jnp.moveaxis(a.reshape(b, h, nc, HG_CHUNK, a.shape[-1]), 2, 0)

    mask = jnp.tril(jnp.ones((HG_CHUNK, HG_CHUNK), dtype=bool))[:, :, None]

    def step(s, inp):
        kc, vc, lf = inp[0], inp[1], inp[2]
        cum = jnp.cumsum(lf, axis=2)
        last = cum[:, :, -1:, :]
        s_new = jnp.exp(last[:, :, 0, :])[..., None] * s + \
            jnp.einsum('bhsd,bhse->bhde', kc * jnp.exp(last - cum), vc)
        if not with_out:
            return s_new, None
        qc = inp[3]
        o_inter = jnp.einsum('bhtd,bhde->bhte', qc * jnp.exp(cum), s)
        diff = cum[:, :, :, None, :] - cum[:, :, None, :, :]
        decay = jnp.exp(jnp.where(mask, diff, -jnp.inf))
        att = jnp.einsum('bhtd,bhsd,bhtsd->bhts', qc, kc, decay)
        return s_new, o_inter + jnp.einsum('bhts,bhse->bhte', att, vc)

    xs = (chunks(k), chunks(v), chunks(log_f)) + ((chunks(q),) if with_out else ())
    s_fin, o = lax.scan(step, s0, xs)
    if with_out:
        o = jnp.moveaxis(o, 0, 2).reshape(b, h, n, v.shape[-1])
    return o, s_fin

def hg_heads(u):
    b, n, _ = u.shape
    return u.reshape(b, n, HG_HEADS, -1).transpose(0, 2, 1, 3).astype(jnp.float32)

def hg_gate(z, lb):
    lb = lb.reshape(HG_HEADS, 1, HG_DK)
    k = (1.0 - lb) * jax.nn.sigmoid(-z)
    log_f = jnp.log(lb + (1.0 - lb) * jax.nn.sigmoid(z))
    return k, log_f

def hg_readout(o, g, gain, dtype):
    b, h, n, dv = o.shape
    y = rmsnorm(o, gain).transpose(0, 2, 1, 3).reshape(b, n, h * dv)
    return (y * jax.nn.silu(g.astype(jnp.float32))).astype(dtype)

def hgrn_group(ux, uc, base_c, lb_dirs, gain, ctx_out):
    b = ux.shape[0]
    vx = hg_heads(col(ux, OFF_I, HG_W))
    qx = hg_heads(col(ux, OFF_HQ, HG_W))
    vc = hg_heads(col(uc, OFF_I, HG_W, base_c))
    qc = hg_heads(col(uc, OFF_HQ, HG_W, base_c)) if ctx_out else None
    s0 = jnp.zeros((b, HG_HEADS, HG_DK, HG_DV), jnp.float32)
    o_x = jnp.zeros_like(vx)
    o_c = jnp.zeros_like(vc) if ctx_out else None
    for d, (off, rev) in enumerate(((OFF_FF, False), (OFF_FB, True))):
        fl = (lambda a: jnp.flip(a, axis=2)) if rev else (lambda a: a)
        kx, lfx = hg_gate(hg_heads(col(ux, off, HG_W)), lb_dirs[d])
        kc, lfc = hg_gate(hg_heads(col(uc, off, HG_W, base_c)), lb_dirs[d])
        oc, s_ctx = hgrn_scan(fl(kc), fl(vc), fl(lfc), s0, fl(qc) if ctx_out else None)
        ox, _ = hgrn_scan(fl(kx), fl(vx), fl(lfx), s_ctx, fl(qx))
        o_x = o_x + fl(ox)
        if ctx_out:
            o_c = o_c + fl(oc)
    out_x = hg_readout(o_x, col(ux, OFF_G, HG_W), gain, ux.dtype)
    out_c = hg_readout(o_c, col(uc, OFF_G, HG_W, base_c), gain, uc.dtype) if ctx_out else None
    return out_x, out_c

def swiglu(h, wg, wu, wd):
    return (jax.nn.silu(h @ wg) * (h @ wu)) @ wd

def first_inputs(seed: int = 0) -> dict:
    key = jax.random.key(seed)
    ks = jax.random.split(key, 18)
    nrm = jax.random.normal
    f32 = jnp.float32
    return {
        "x": nrm(ks[0], (BATCH, SEQ, D_MODEL), f32),
        "c": nrm(ks[1], (BATCH, D_MODEL), f32),
        "ctx": nrm(ks[2], (BATCH, CTX_LEN, D_MODEL), f32),
        "c_ctx": nrm(ks[3], (D_MODEL,), f32),
        "w_ada": nrm(ks[4], (DEPTH, D_MODEL, 6 * D_MODEL), f32) * D_MODEL ** -0.5,
        "b_ada": nrm(ks[5], (DEPTH, 6 * D_MODEL), f32) * 0.02,
        "w_in": nrm(ks[6], (DEPTH, D_MODEL, PROJ_W), f32) * D_MODEL ** -0.5,
        "w_four": nrm(ks[7], (DEPTH, FOURIER_W, FOURIER_W), f32) * FOURIER_W ** -0.5,
        "q_norm": 1.0 + 0.02 * nrm(ks[8], (DEPTH, HEAD_DIM), f32),
        "k_norm": 1.0 + 0.02 * nrm(ks[9], (DEPTH, HEAD_DIM), f32),
        "hg_lb_logits": 0.5 * nrm(ks[10], (2, DEPTH, HG_W), f32),
        "hg_norm": 1.0 + 0.02 * nrm(ks[11], (DEPTH, HG_DV), f32),
        "w_out": nrm(ks[12], (DEPTH, MIX_W, D_MODEL), f32) * MIX_W ** -0.5,
        "w_gate": nrm(ks[13], (DEPTH, D_MODEL, D_FF), f32) * D_MODEL ** -0.5,
        "w_up": nrm(ks[14], (DEPTH, D_MODEL, D_FF), f32) * D_MODEL ** -0.5,
        "w_down": nrm(ks[15], (DEPTH, D_FF, D_MODEL), f32) * D_FF ** -0.5,
        "final_norm": 1.0 + 0.02 * nrm(ks[16], (D_MODEL,), f32),
    }

def first_block(x, c, ctx, c_ctx, w_ada, b_ada, w_in, w_four, q_norm, k_norm,
              hg_lb_logits, hg_norm, w_out, w_gate, w_up, w_down, final_norm):
    d = D_MODEL
    tabs = axial_rope_tables(x.shape[1])
    silu_c = jax.nn.silu(c)
    silu_cc = jax.nn.silu(c_ctx)
    lb_sm = jax.nn.softmax(hg_lb_logits.astype(jnp.float32), axis=1)
    lb_all = jnp.cumsum(lb_sm, axis=1) - lb_sm[:, :1]
    for l in range(DEPTH):
        ctx_out = l < DEPTH - 1
        mod = silu_c @ w_ada[l] + b_ada[l]
        sh_a, sc_a, g_a, sh_f, sc_f, g_f = jnp.split(mod[:, None, :], 6, axis=-1)
        n_c = 6 * d if ctx_out else 2 * d
        mc = jnp.split(silu_cc @ w_ada[l][:, :n_c] + b_ada[l][:n_c], n_c // d)
        hx = rmsnorm(x) * (1 + sc_a) + sh_a
        hc = rmsnorm(ctx) * (1 + mc[1]) + mc[0]
        ux = hx @ w_in[l]
        base_c = 0 if ctx_out else OFF_K
        uc = hc @ (w_in[l] if ctx_out else w_in[l][:, OFF_K:OFF_HQ])
        fx = fourier_mix(col(ux, OFF_FOURIER, FOURIER_W), w_four[l])
        ax, ac = attention_group(ux, uc, base_c, q_norm[l], k_norm[l], tabs, ctx_out)
        rx, rc = hgrn_group(ux, uc, base_c, lb_all[:, l], hg_norm[l], ctx_out)
        x = x + g_a * (jnp.concatenate([fx, ax, rx], axis=-1) @ w_out[l])
        x = x + g_f * swiglu(rmsnorm(x) * (1 + sc_f) + sh_f, w_gate[l], w_up[l], w_down[l])
        if ctx_out:
            fc = fourier_mix(col(uc, OFF_FOURIER, FOURIER_W), w_four[l])
            ctx = ctx + mc[2] * (jnp.concatenate([fc, ac, rc], axis=-1) @ w_out[l])
            ctx = ctx + mc[5] * swiglu(rmsnorm(ctx) * (1 + mc[4]) + mc[3], w_gate[l], w_up[l], w_down[l])
    return rmsnorm(x, final_norm)


N_EVEN = (DEPTH + 1) // 2
N_ODD = DEPTH // 2
D_FF_2 = 2816
NORM_EPS = 1e-6

ATTN_HEADS = 8
ATTN_WIDTH = ATTN_HEADS * HEAD_DIM
ROT_DIM = HEAD_DIM // 4
ROPE_THETA_2 = 500000.0
MOBA_BLOCK = 256
MOBA_TOPK = 3
MOBA_Q_CHUNK = 32

LRU_WIDTH = 512
LRU_HEADS = 8
LRU_HEAD_DIM = LRU_WIDTH // LRU_HEADS
LRU_CONV = 4
LRU_C = 8.0

AB_IN = 3 * ATTN_WIDTH + 2 * LRU_WIDTH
AB_OUT = ATTN_WIDTH + LRU_WIDTH

SC_WIDTH = D_MODEL
SC_CONV = 3


def rms_norm(x, g):
    xf = x.astype(jnp.float32)
    y = xf * lax.rsqrt(jnp.mean(xf * xf, axis=-1, keepdims=True) + NORM_EPS) * g.astype(jnp.float32)
    return y.astype(x.dtype)

def swiglu_2(h, w_gate, w_up, w_down):
    return (jax.nn.silu(h @ w_gate) * (h @ w_up)) @ w_down

def causal_depthwise_conv(x, w):
    k, c = w.shape
    return lax.conv_general_dilated(
        x, w[:, None, :].astype(x.dtype), window_strides=(1,), padding=[(k - 1, 0)],
        dimension_numbers=("NWC", "WIO", "NWC"), feature_group_count=c)

def partial_rope(x, pos):
    half = ROT_DIM // 2
    inv_freq = ROPE_THETA_2 ** (-jnp.arange(0, ROT_DIM, 2, dtype=jnp.float32) / ROT_DIM)
    ang = pos[:, None] * inv_freq[None, :]
    cos = jnp.cos(ang)[None, :, None, :]
    sin = jnp.sin(ang)[None, :, None, :]
    xf = x.astype(jnp.float32)
    x1, x2, rest = xf[..., :half], xf[..., half:ROT_DIM], xf[..., ROT_DIM:]
    out = jnp.concatenate([x1 * cos - x2 * sin, x2 * cos + x1 * sin, rest], axis=-1)
    return out.astype(x.dtype)

def moba_attention(q, k, v):
    b, s, h, hd = q.shape
    n_blk = -(-s // MOBA_BLOCK)
    sp = n_blk * MOBA_BLOCK
    pad = ((0, 0), (0, sp - s), (0, 0), (0, 0))
    qt = jnp.pad(q, pad).transpose(0, 2, 1, 3)
    kt = jnp.pad(k, pad).transpose(0, 2, 1, 3)
    vt = jnp.pad(v, pad).transpose(0, 2, 1, 3)
    kb = kt.reshape(b, h, n_blk, MOBA_BLOCK, hd)
    vb = vt.reshape(b, h, n_blk, MOBA_BLOCK, hd)
    kmean = jnp.mean(kb.astype(jnp.float32), axis=3)
    n_sel = min(MOBA_TOPK, n_blk - 1)
    scale = hd ** -0.5
    blk_ids = jnp.arange(n_blk)
    bi = jnp.arange(b)[:, None, None]
    hi = jnp.arange(h)[None, :, None]
    neg = jnp.float32(-1e30)

    def chunk(c):
        start = c * MOBA_Q_CHUNK
        own = start // MOBA_BLOCK
        qc = lax.dynamic_slice_in_dim(qt, start, MOBA_Q_CHUNK, axis=2)
        qpos = start + jnp.arange(MOBA_Q_CHUNK)
        k_own = lax.dynamic_index_in_dim(kb, own, axis=2, keepdims=False)
        v_own = lax.dynamic_index_in_dim(vb, own, axis=2, keepdims=False)
        kpos = own * MOBA_BLOCK + jnp.arange(MOBA_BLOCK)
        s_own = jnp.einsum("bhqd,bhkd->bhqk", qc, k_own).astype(jnp.float32) * scale
        s_own = jnp.where(kpos[None, :] <= qpos[:, None], s_own, neg)
        logits = [s_own]
        vals = [v_own]
        if n_sel > 0:
            g = jnp.einsum("bhqd,bhnd->bhqn", qc.astype(jnp.float32), kmean)
            g = jnp.where(blk_ids < own, g, neg)
            _, idx = lax.top_k(g, n_sel)
            valid = idx < own
            for j in range(n_sel):
                ks = kb[bi, hi, idx[..., j]]
                vs = vb[bi, hi, idx[..., j]]
                sj = jnp.einsum("bhqd,bhqkd->bhqk", qc, ks).astype(jnp.float32) * scale
                logits.append(jnp.where(valid[..., j][..., None], sj, neg))
                vals.append(vs)
        p = jax.nn.softmax(jnp.concatenate(logits, axis=-1), axis=-1)
        p = p.astype(v.dtype)
        out = jnp.einsum("bhqk,bhkd->bhqd", p[..., :MOBA_BLOCK], vals[0])
        for j in range(1, n_sel + 1):
            pj = p[..., j * MOBA_BLOCK:(j + 1) * MOBA_BLOCK]
            out = out + jnp.einsum("bhqk,bhqkd->bhqd", pj, vals[j])
        return out

    outs = lax.map(chunk, jnp.arange(sp // MOBA_Q_CHUNK))
    outs = outs.transpose(1, 0, 3, 2, 4).reshape(b, sp, h, hd)[:, :s]
    return outs.reshape(b, s, h * hd)

def rg_lru(xc, wa, ba, wx, bx, lam):
    b, s, w = xc.shape
    xf = xc.astype(jnp.float32).reshape(b, s, LRU_HEADS, LRU_HEAD_DIM)
    r = jax.nn.sigmoid(jnp.einsum("bshi,hij->bshj", xf, wa.astype(jnp.float32)) + ba.astype(jnp.float32))
    i = jax.nn.sigmoid(jnp.einsum("bshi,hij->bshj", xf, wx.astype(jnp.float32)) + bx.astype(jnp.float32))
    log_a = -LRU_C * r * jax.nn.softplus(-lam.astype(jnp.float32)).reshape(LRU_HEADS, LRU_HEAD_DIM)
    a = jnp.exp(log_a)
    u = jnp.sqrt(-jnp.expm1(2.0 * log_a)) * (i * xf)
    a = a.reshape(b, s, w)
    u = u.reshape(b, s, w)

    def combine(e1, e2):
        a1, u1 = e1
        a2, u2 = e2
        return a1 * a2, a2 * u1 + u2

    _, hseq = lax.associative_scan(combine, (a, u), axis=1)
    return hseq.astype(xc.dtype)

def second_inputs(seed: int = 0) -> dict:
    key = jax.random.key(seed)
    ks = jax.random.split(key, 24)
    f32 = jnp.float32

    def nrm(k, shape, fan_in):
        return jax.random.normal(k, shape, f32) * (fan_in ** -0.5)

    x = jax.random.normal(ks[0], (BATCH, SEQ, D_MODEL), f32)
    ffn1_w_gate = nrm(ks[1], (DEPTH, D_MODEL, D_FF_2), D_MODEL)
    ffn1_w_up = nrm(ks[2], (DEPTH, D_MODEL, D_FF_2), D_MODEL)
    ffn1_w_down = nrm(ks[3], (DEPTH, D_FF_2, D_MODEL), D_FF_2)
    ffn2_w_gate = nrm(ks[4], (DEPTH, D_MODEL, D_FF_2), D_MODEL)
    ffn2_w_up = nrm(ks[5], (DEPTH, D_MODEL, D_FF_2), D_MODEL)
    ffn2_w_down = nrm(ks[6], (DEPTH, D_FF_2, D_MODEL), D_FF_2)
    norm_pre = 1.0 + 0.05 * jax.random.normal(ks[7], (DEPTH, 3, D_MODEL), f32)
    norm_post = 1.0 + 0.05 * jax.random.normal(ks[8], (DEPTH, 3, D_MODEL), f32)
    ab_w_in = nrm(ks[9], (N_EVEN, D_MODEL, AB_IN), D_MODEL)
    ab_w_out = nrm(ks[10], (N_EVEN, AB_OUT, D_MODEL), AB_OUT)
    lru_conv_w = nrm(ks[11], (N_EVEN, LRU_CONV, LRU_WIDTH), LRU_CONV)
    lru_conv_b = 0.01 * jax.random.normal(ks[12], (N_EVEN, LRU_WIDTH), f32)
    lru_gate_a_w = nrm(ks[13], (N_EVEN, LRU_HEADS, LRU_HEAD_DIM, LRU_HEAD_DIM), LRU_HEAD_DIM)
    lru_gate_a_b = 0.01 * jax.random.normal(ks[14], (N_EVEN, LRU_HEADS, LRU_HEAD_DIM), f32)
    lru_gate_x_w = nrm(ks[15], (N_EVEN, LRU_HEADS, LRU_HEAD_DIM, LRU_HEAD_DIM), LRU_HEAD_DIM)
    lru_gate_x_b = 0.01 * jax.random.normal(ks[16], (N_EVEN, LRU_HEADS, LRU_HEAD_DIM), f32)
    a_c = jax.random.uniform(ks[17], (N_EVEN, LRU_WIDTH), f32, 0.9, 0.999)
    a0 = a_c ** (1.0 / LRU_C)
    lru_lambda = jnp.log(a0) - jnp.log1p(-a0)
    c_w_in = nrm(ks[18], (N_ODD, D_MODEL, 3 * SC_WIDTH), D_MODEL)
    c_conv_w = nrm(ks[19], (N_ODD, SC_CONV, SC_WIDTH), SC_CONV)
    c_w_out = nrm(ks[20], (N_ODD, SC_WIDTH, D_MODEL), SC_WIDTH)
    return {
        "x": x,
        "ffn1_w_gate": ffn1_w_gate, "ffn1_w_up": ffn1_w_up, "ffn1_w_down": ffn1_w_down,
        "ffn2_w_gate": ffn2_w_gate, "ffn2_w_up": ffn2_w_up, "ffn2_w_down": ffn2_w_down,
        "norm_pre": norm_pre, "norm_post": norm_post,
        "ab_w_in": ab_w_in, "ab_w_out": ab_w_out,
        "lru_conv_w": lru_conv_w, "lru_conv_b": lru_conv_b,
        "lru_gate_a_w": lru_gate_a_w, "lru_gate_a_b": lru_gate_a_b,
        "lru_gate_x_w": lru_gate_x_w, "lru_gate_x_b": lru_gate_x_b,
        "lru_lambda": lru_lambda,
        "c_w_in": c_w_in, "c_conv_w": c_conv_w, "c_w_out": c_w_out,
    }

def second_block(x, ffn1_w_gate, ffn1_w_up, ffn1_w_down, ffn2_w_gate, ffn2_w_up, ffn2_w_down,
              norm_pre, norm_post, ab_w_in, ab_w_out, lru_conv_w, lru_conv_b,
              lru_gate_a_w, lru_gate_a_b, lru_gate_x_w, lru_gate_x_b, lru_lambda,
              c_w_in, c_conv_w, c_w_out):
    b, s, d = x.shape
    pos = jnp.arange(s, dtype=jnp.float32)
    for l in range(DEPTH):
        hdn = swiglu_2(rms_norm(x, norm_pre[l, 0]), ffn1_w_gate[l], ffn1_w_up[l], ffn1_w_down[l])
        x = x + 0.5 * rms_norm(hdn, norm_post[l, 0])

        h = rms_norm(x, norm_pre[l, 1])
        if l % 2 == 0:
            e = l // 2
            p = h @ ab_w_in[e]
            q = p[..., :ATTN_WIDTH].reshape(b, s, ATTN_HEADS, HEAD_DIM)
            k = p[..., ATTN_WIDTH:2 * ATTN_WIDTH].reshape(b, s, ATTN_HEADS, HEAD_DIM)
            v = p[..., 2 * ATTN_WIDTH:3 * ATTN_WIDTH].reshape(b, s, ATTN_HEADS, HEAD_DIM)
            lru_x = p[..., 3 * ATTN_WIDTH:3 * ATTN_WIDTH + LRU_WIDTH]
            lru_g = p[..., 3 * ATTN_WIDTH + LRU_WIDTH:]
            attn = moba_attention(partial_rope(q, pos), partial_rope(k, pos), v)
            xc = causal_depthwise_conv(lru_x, lru_conv_w[e]) + lru_conv_b[e]
            rec = rg_lru(xc, lru_gate_a_w[e], lru_gate_a_b[e], lru_gate_x_w[e], lru_gate_x_b[e],
                         lru_lambda[e]) * jax.nn.gelu(lru_g)
            mix = jnp.concatenate([attn, rec], axis=-1) @ ab_w_out[e]
        else:
            o = l // 2
            p = h @ c_w_in[o]
            gate_b = p[..., :SC_WIDTH]
            gate_c = p[..., SC_WIDTH:2 * SC_WIDTH]
            xt = p[..., 2 * SC_WIDTH:]
            mix = (gate_b * causal_depthwise_conv(gate_c * xt, c_conv_w[o])) @ c_w_out[o]
        x = x + rms_norm(mix, norm_post[l, 1])

        hdn = swiglu_2(rms_norm(x, norm_pre[l, 2]), ffn2_w_gate[l], ffn2_w_up[l], ffn2_w_down[l])
        x = x + 0.5 * rms_norm(hdn, norm_post[l, 2])
    return x


def setup_inputs(seed=0):
    out = dict(first_inputs(seed))
    for name, value in second_inputs(seed + 1).items():
        if name != "x":
            out[name + "_2"] = value
    return out


def reference(
    x, c, ctx, c_ctx, w_ada, b_ada, w_in, w_four, q_norm, k_norm, hg_lb_logits, hg_norm, w_out,
    w_gate, w_up, w_down, final_norm, ffn1_w_gate_2, ffn1_w_up_2, ffn1_w_down_2, ffn2_w_gate_2,
    ffn2_w_up_2, ffn2_w_down_2, norm_pre_2, norm_post_2, ab_w_in_2, ab_w_out_2, lru_conv_w_2,
    lru_conv_b_2, lru_gate_a_w_2, lru_gate_a_b_2, lru_gate_x_w_2, lru_gate_x_b_2, lru_lambda_2,
    c_w_in_2, c_conv_w_2, c_w_out_2,
):
    x = first_block(
        x, c, ctx, c_ctx, w_ada, b_ada, w_in, w_four, q_norm, k_norm, hg_lb_logits, hg_norm,
        w_out, w_gate, w_up, w_down, final_norm,
    )
    return second_block(
        x, ffn1_w_gate_2, ffn1_w_up_2, ffn1_w_down_2, ffn2_w_gate_2, ffn2_w_up_2, ffn2_w_down_2,
        norm_pre_2, norm_post_2, ab_w_in_2, ab_w_out_2, lru_conv_w_2, lru_conv_b_2,
        lru_gate_a_w_2, lru_gate_a_b_2, lru_gate_x_w_2, lru_gate_x_b_2, lru_lambda_2, c_w_in_2,
        c_conv_w_2, c_w_out_2,
    )


_drawn_inputs = setup_inputs


def setup_inputs(seed=0):
    import zlib

    import numpy as np

    out = dict(_drawn_inputs(seed))
    spreads = {}
    factors = {'q_norm': 8.0,
     'k_norm': 8.0,
     'hg_norm': 4.688,
     'lru_gate_a_b_2': 39.458,
     'lru_gate_x_b_2': 8.0}
    for name, (base, spread) in spreads.items():
        noise = np.random.default_rng([zlib.crc32(name.encode()), seed]).standard_normal(out[name].shape)
        drawn = base * np.exp(spread * noise) if base else spread * noise
        out[name] = __import__('jax').numpy.asarray(drawn.astype(out[name].dtype))
    for name, factor in factors.items():
        out[name] = (out[name] * factor).astype(out[name].dtype)
    return out
```

```python
from contextlib import ExitStack

import numpy as np

import concourse.bass as bass
from concourse import mybir

F32 = mybir.dt.float32
F32R = mybir.dt.float32r
U32 = mybir.dt.uint32
ALU = mybir.AluOpType
ACT = mybir.ActivationFunctionType
AX_X = mybir.AxisListType.X

P = 128
D = 1024
NC = D // P
SEQ, CTX = 512, 256
TOK = SEQ + CTX
BANK = 512
DEPTH = 2
HD = 64
DFF = 2816
GROUPS = [8, 8, 6]
PANEL = NC * 2 * P
EPS = 1e-6
MOD = 6 * NC
SH_A, SC_A, G_A, SH_F, SC_F, G_F = (NC * j for j in range(6))
UF, UQ, UK, UV, UFF, UFB, UI, UHQ, UG, UN = 0, 2, 6, 7, 8, 10, 12, 14, 16, 18
LEVELS = 7
SCALE = HD ** -0.5
NEG = -1e30


def column_map():
    at, n = {}, 0
    for name, width in (
        ("b_ada", DEPTH * MOD), ("q_norm", DEPTH), ("k_norm", DEPTH), ("hg_norm", DEPTH), ("lb", 2 * DEPTH * 2),
        ("final", NC), ("pre", DEPTH * 3 * NC), ("post", DEPTH * 3 * NC), ("conv_w", 4 * 4), ("conv_b", 4),
        ("ba", 4), ("bx", 4), ("lam", 4), ("c_conv", 3 * NC),
    ):
        at[name] = n
        n += width
    return at, n


COL, NCOL = column_map()


class Ticket:

    def __init__(self, sem, c, k=0, i=None):
        self.sem, self.c, self.k, self.i = sem, c, k, i

    def value(self):
        return self.i * self.k + self.c if self.k else self.c

    def at(self, step):
        return Ticket(self.sem, self.c + self.k * step)


class Carry:

    def __init__(self, book):
        self.t, self.stamp = [], None
        book.carries.append(self)
        self.book = book

    def set(self, *t):
        self.t, self.stamp = list(t), self.book.loop

    def add(self, *t):
        if self.stamp is not self.book.loop:
            self.t = []
        self.t, self.stamp = self.t + list(t), self.book.loop


class Book:
    def __init__(self, nc):
        self.nc, self.engines, self.carries, self.loop, self.dry = nc, [], [], None, False

    def repeat(self, steps, body):
        if steps == 1:
            body(0)
            return
        before = [(c, list(c.t), c.stamp) for c in self.carries]
        base = {e: e.n for e in self.engines}
        known = {e: dict(e.known) for e in self.engines}
        self.loop, self.dry = {"guards": [], "final": {}, "per": {}, "i": None}, True
        loop = self.loop
        body(0)
        per = {e.sem: e.n - base[e] for e in self.engines}
        final = {c: list(c.t) for c in self.carries if c.stamp is loop}
        for c, t, stamp in before:
            c.t, c.stamp = t, stamp
        for e in self.engines:
            e.n, e.known = base[e], known[e]
        self.loop, self.dry = None, False
        for engine, carry in loop["guards"]:
            if carry in final:
                engine.wait(*carry.t)
        for e in self.engines:
            e.flush()
        with self.nc.Fori(0, steps) as i:
            loop.update(per=per, final=final, i=i)
            self.loop = loop
            body(i)
            for e in self.engines:
                e.flush()
        self.loop = None
        for c in self.carries:
            if c.stamp is loop:
                c.t, c.stamp = [t.at(steps - 1) for t in c.t], None
        for e in self.engines:
            assert e.n == base[e] + per[e.sem]
            e.n = base[e] + steps * per[e.sem]
            e.near = {}


class Engine:

    def __init__(self, book, engine, sem):
        self.book, self.e, self.sem, self.n, self.known, self.near = book, engine, sem, 0, {}, {}
        self.pending = []
        book.engines.append(self)

    def do(self, op, *args, inc=True, sem=None, **kw):
        if not self.book.dry:
            self.flush(op.__name__ in ("activation", "copy_predicated"))
            ins = op(*args, **kw)
            if sem is not None:
                ins.then_inc(sem, 1)
            elif inc:
                ins.then_inc(self.sem, 1)
        if sem is not None or not inc:
            return None
        self.n += 1
        loop = self.book.loop
        if loop is None:
            return Ticket(self.sem, self.n)
        return Ticket(self.sem, self.n, loop["per"].get(self.sem, 0), loop["i"])

    def wait(self, *tickets):
        if self.book.dry:
            return
        for t in tickets:
            if t is None:
                continue
            seen = self.near.get(t.sem) if t.k else self.known.get(t.sem)
            if t.k and (seen is None or seen[0] is not self.book.loop or seen[1] < t.c) or \
                    not t.k and (seen is None or seen < t.c):
                self.pending.append(t)
                if t.k:
                    self.near[t.sem] = (self.book.loop, t.c)
                else:
                    self.known[t.sem] = t.c

    def flush(self, fence=False):
        for t in self.pending:
            self.e.wait_ge(t.sem, t.value())
        if fence and any(t.k for t in self.pending):
            self.e.nop(nofuse=True)
        self.pending = []

    def take(self, carry):
        loop = self.book.loop
        if loop is None or carry.stamp is loop:
            self.wait(*carry.t)
        elif self.book.dry:
            loop["guards"].append((self, carry))
        elif carry in loop["final"]:
            self.wait(*[Ticket(t.sem, t.c - loop["per"][t.sem], loop["per"][t.sem], loop["i"])
                        if t.sem in loop["per"] else t for t in loop["final"][carry]])
        else:
            self.wait(*carry.t)


def ds(start, n):
    return slice(start, start + n) if isinstance(start, int) else bass.ds(start, n)


def program(nc, xT, cvec, cols, panels, ada_panels, w_four, lru_gates, mats, rope1, rope2, dft_x, dft_c, masks,
            causal, out, dbg=None, stop=None):
    n_panels = panels.shape[0] if stop is None else \
        dict(mix0=14, ffn0=48, mix1=62, ffn1=96, b00=130, b01=144, b02=178, b10=212, b11=228)[stop]
    stack = ExitStack()
    with stack:
        def sb(name, shape, dt=F32, scope=stack):
            return scope.enter_context(nc.sbuf_tensor(name, shape, dt))

        def semaphore(name):
            return stack.enter_context(nc.semaphore(name))

        book = Book(nc)
        T = Engine(book, nc.tensor, semaphore("tensor_done"))
        A = Engine(book, nc.scalar, semaphore("scalar_done"))
        V = Engine(book, nc.vector, semaphore("vector_done"))
        G = Engine(book, nc.gpsimd, semaphore("gpsimd_done"))
        SP = nc.sync
        te, ac, ve, gp = nc.tensor, nc.scalar, nc.vector, nc.gpsimd
        raw_in = [semaphore(f"panel_landed_{s}") for s in range(2)]
        high_done, low_done = semaphore("panel_high"), semaphore("panel_low")
        ada_in = [semaphore(f"ada_landed_{s}") for s in range(2)]

        X = sb("X", [P, NC, TOK])
        raw = sb("raw", [P, 2, PANEL])
        WH = [sb(f"WH{s}", [P, NC, 2 * P], F32R) for s in range(2)]
        WL = [sb(f"WL{s}", [P, NC, 2 * P], F32R) for s in range(2)]
        C = sb("C", [P, NCOL])
        M = sb("M", [P, mats.shape[1], P])
        mod = sb("mod", [P, DEPTH, MOD, 2])
        SQ = [sb(f"SQ{s}", [P, TOK]) for s in range(2)]
        RS = sb("RS", [P, TOK])
        PS = stack.enter_context(nc.psum_tensor("PS", [P, 8, BANK], F32))
        bank = [Carry(book) for _ in range(8)]
        c_SQ, c_RS, c_X, c_XN = [Carry(book), Carry(book)], Carry(book), Carry(book), Carry(book)
        ONES, EYE, BO, RQ, D0, D1, R0, R1, R2, DC, DS = (M[:, j, :] for j in range(11))
        stack.enter_context(nc.Block())

        loads = [0]

        def load(eng, *pairs):
            sem = semaphore(f"load_{loads[0]}")
            loads[0] += 1
            eng.flush()
            for dst, src in pairs:
                eng.e.dma_start(dst, src).then_inc(sem, 16)
            return Ticket(sem, 16 * len(pairs))

        def col(name, j=0, n=1):
            return C[:, ds(COL[name] + j, n)]

        def everyone(*engines):
            return [Ticket(e.sem, e.n) for e in (engines or (T, A, V, G))]

        for s in range(2):
            SP.dma_start(raw[:, s, :], panels[s]).then_inc(raw_in[s], 16)
        with nc.sync.Fori(1, n_panels // 2) as i:
            for s in range(2):
                SP.wait_ge(low_done, i * 2 + (s - 1))
                SP.dma_start(raw[:, s, :], panels[bass.ds(i * 2 + s, 1)].rearrange("a p n -> p (a n)"))\
                    .then_inc(raw_in[s], 16)

        t_const = load(G, (C[:], cols), (M[:], mats))
        t_cv_x = load(A, (X[:, :, :], xT))

        split_n = [0]
        used = [Carry(book), Carry(book)]

        def split(offset=0):
            n = split_n[0] + offset
            loop = book.loop
            k, i = (1, loop["i"]) if loop else (0, None)
            s = n % 2
            A.wait(Ticket(raw_in[s], 16 * (n // 2 + 1), 16 * k, i))
            A.take(used[s])
            A.do(ac.activation, WH[s].rearrange("p k n -> p (k n)"), raw[:, s, :], ACT.Copy, sem=high_done)
            V.wait(Ticket(high_done, n + 1, 2 * k, i))
            V.do(ve.tensor_tensor, WL[s].rearrange("p k n -> p (k n)"), raw[:, s, :],
                 WH[s].bitcast(F32).rearrange("p k n -> p (k n)"), ALU.subtract, sem=low_done)

        def panel(n_local, nk, rhs, ready, ctx, epilogue, p, last):
            n = split_n[0] + n_local
            s = n % 2
            loop = book.loop
            k2, i = (2, loop["i"]) if loop else (0, None)
            if not last:
                split(n_local + 1)
            XH, XL = rhs
            for j in range(2):
                T.wait(Ticket(low_done, n + 1, k2, i))
                T.take(bank[j])
                if ctx:
                    T.take(bank[2 + j])
                for k in range(nk):
                    T.wait(*ready(k))
                    for q, (w, x) in enumerate(((WH, XH), (WH, XL), (WL, XH))):
                        st, sp = k == 0 and q == 0, k == nk - 1 and q == 2
                        lhsT = w[s][:, k, j * P:(j + 1) * P]
                        t = T.do(te.matmul, PS[:, j, :], lhsT, x[:, k, 0:SEQ], start=st, stop=sp, inc=sp and not ctx)
                        if ctx:
                            t = T.do(te.matmul, PS[:, 2 + j, 0:CTX], lhsT, x[:, k, SEQ:TOK], start=st, stop=sp,
                                     inc=sp)
                bank[j].set(t)
                if ctx:
                    bank[2 + j].set(t)
                if j == 1:
                    used[s].set(t)
                epilogue(p * 2 + j, j, t)

        def gemm(n, nk, rhs, ready, ctx, epilogue, final=False, first=0):
            pairs = n // 2 - (1 if final else 0)
            if pairs == 1:
                for u in range(2):
                    panel(u, nk, rhs, ready, ctx, epilogue, first + u, False)
            elif pairs > 1:
                def body(i):
                    for u in range(2):
                        panel(u, nk, rhs, ready, ctx, epilogue, i * 2 + (first + u), False)
                book.repeat(pairs, body)
            split_n[0] += 2 * pairs
            left = n - 2 * pairs
            for u in range(left):
                panel(0, nk, rhs, ready, ctx, epilogue, first + 2 * pairs + u, final and u == left - 1)
                split_n[0] += 1

        def spans(ctx):
            return [(0, SEQ, 0), (SEQ, TOK, 1)] if ctx else [(0, SEQ, 0)]

        def mean_square(src, n, ctx):
            N = TOK if ctx else SEQ
            T.take(bank[6])
            T.take(bank[7])
            for c in range(n):
                u = c % 2
                A.take(c_SQ[u])
                A.take(c_X)
                t = A.do(ac.activation, SQ[u][:, 0:N], src(c)[:, 0:N], ACT.Square)
                T.wait(t)
                for a, b, q in spans(ctx):
                    t = T.do(te.matmul, PS[:, 6 + q, 0:b - a], ONES, SQ[u][:, a:b], start=c == 0, stop=c == n - 1)
                c_SQ[u].set(t)
            inverse_root(6, N, t)

        def inverse_root(b, N, t):
            V.wait(t)
            V.take(c_RS)
            flat = PS[:, b:b + 2, :].rearrange("p b n -> p (b n)")
            t = V.do(ve.tensor_scalar, RS[:, 0:N], flat[:, 0:N], EPS, None, ALU.add)
            bank[b].set(t)
            bank[b + 1].set(t)
            A.wait(t)
            t = A.do(ac.activation, RS[:, 0:N], RS[:, 0:N], ACT.Sqrt)
            V.wait(t)
            t = V.do(ve.reciprocal, RS[:, 0:N], RS[:, 0:N])
            c_RS.set(t)
            return t

        def normed(XH, XL, ctx, gain, shift, free):
            tickets = []
            V.wait(*free)
            A.wait(*free)
            for c in range(NC):
                u = c % 2
                V.take(c_SQ[u])
                V.take(c_RS)
                V.take(c_X)
                for a, b, q in spans(ctx):
                    t = V.do(ve.scalar_tensor_tensor, SQ[u][:, a:b], X[:, c, a:b], gain(c, q), RS[:, a:b],
                             ALU.mult, ALU.mult)
                A.wait(t)
                for a, b, q in spans(ctx):
                    t = A.do(ac.activation, XH[:, c, a:b], SQ[u][:, a:b], ACT.Identity,
                             bias=shift(c, q) if shift else 0.0)
                V.wait(t)
                for a, b, q in spans(ctx):
                    t = V.do(ve.scalar_tensor_tensor, XL[:, c, a:b], SQ[u][:, a:b], shift(c, q) if shift else 0.0,
                             XH[:, c, a:b].bitcast(F32), ALU.add, ALU.subtract)
                c_SQ[u].set(t)
                tickets.append(t)
            c_RS.add(t)
            c_X.add(t)
            return lambda k: [tickets[k]]

        def split_chunks(XH, XL, src, n, ctx, src_ready, free):
            tickets = []
            N = TOK if ctx else SEQ
            A.wait(*free)
            V.wait(*free)
            A.wait(*src_ready)
            V.wait(*src_ready)
            for c in range(n):
                t = A.do(ac.activation, XH[:, c, 0:N], src(c)[:, 0:N], ACT.Copy)
                V.wait(t)
                tickets.append(V.do(ve.tensor_tensor, XL[:, c, 0:N], src(c)[:, 0:N],
                                    XH[:, c, 0:N].bitcast(F32), ALU.subtract))
            return lambda k: [tickets[k]]

        def modulation(l, cv, t_cv):
            scope = ExitStack()
            ada_raw = sb(f"ada_raw_{l}", [P, 2, NC, 2 * P], F32, scope)
            A.wait(*everyone())

            def body(i):
                for s in range(2):
                    loop = book.loop
                    k, it = (16, loop["i"]) if loop else (0, None)
                    A.take(c_ada[s])
                    if not book.dry:
                        A.flush()
                        ac.dma_start(ada_raw[:, s, :, :].rearrange("p k n -> p (k n)"),
                                     ada_panels[bass.ds(i * 2 + (l * MOD // 2 + s), 1)]
                                     .rearrange("a p n -> p (a n)")).then_inc(ada_in[s], 16)
                    T.wait(Ticket(ada_in[s], 16 * (l * MOD // 4 + 1), k, it))
                    T.wait(t_cv)
                    T.take(bank[4 + s])
                    for j in range(2):
                        for k_ in range(NC):
                            t = T.do(te.matmul, PS[:, 4 + s, j * 2:j * 2 + 2], ada_raw[:, s, k_, j * P:(j + 1) * P],
                                     cv[:, k_, :], start=k_ == 0, stop=k_ == NC - 1, inc=k_ == NC - 1 and j == 1)
                    c_ada[s].set(t)
                    V.wait(t)
                    V.wait(t_const)
                    bias = C[:, ds(i * 4 + (COL["b_ada"] + l * MOD + 2 * s), 2)].unsqueeze(2).broadcast_to([P, 2, 2])
                    t = V.do(ve.tensor_tensor, mod[:, l, ds(i * 4 + 2 * s, 2), :],
                             PS[:, 4 + s, 0:4].rearrange("p (a b) -> p a b", a=2), bias, ALU.add)
                    bank[4 + s].set(t)
            book.repeat(MOD // 4, body)
            t = Ticket(V.sem, V.n)
            V.wait(t)
            for sc in (SC_A, SC_F):
                t = V.do(ve.tensor_scalar, mod[:, l, sc:sc + NC, :], mod[:, l, sc:sc + NC, :], 1.0, None, ALU.add)
            A.wait(t)
            V.wait(t)
            scope.close()

        c_ada = [Carry(book), Carry(book)]

        def ffn(tag, ctx, gain, shift, down, final=False):
            N = TOK if ctx else SEQ
            with ExitStack() as scope:
                XH = sb(f"XH_{tag}", [P, NC, N], F32R, scope)
                XL = sb(f"XL_{tag}", [P, NC, N], F32R, scope)
                HH = sb(f"HH_{tag}", [P, NC, N], F32R, scope)
                HL = sb(f"HL_{tag}", [P, NC, N], F32R, scope)
                GA = [sb(f"GA{s}_{tag}", [P, N], F32, scope) for s in range(1)]
                mean_square(lambda c: X[:, c, :], NC, ctx)
                ready = normed(XH, XL, ctx, gain, shift, everyone())
                c_GA, c_hid = Carry(book), Carry(book)
                for g, nk in enumerate(GROUPS):
                    hid = Carry(book)

                    def gate_up(c, j, t, hid=hid):
                        if j == 0:
                            A.wait(t)
                            A.take(c_GA)
                            for a, b, q in spans(ctx):
                                ta = A.do(ac.activation, GA[0][:, a:b], PS[:, 2 * q, 0:b - a], ACT.Silu)
                                bank[2 * q].set(ta)
                            c_GA.set(ta)
                            return
                        m = c_of(c)
                        V.wait(t)
                        V.take(c_GA)
                        for a, b, q in spans(ctx):
                            tv = V.do(ve.tensor_tensor, GA[0][:, a:b], PS[:, 2 * q + 1, 0:b - a], GA[0][:, a:b],
                                      ALU.mult)
                            bank[2 * q + 1].set(tv)
                        A.wait(tv)
                        ta = A.do(ac.activation, HH[:, ds(m, 1), :], GA[0][:, :].unsqueeze(1), ACT.Copy)
                        V.wait(ta)
                        tv = V.do(ve.tensor_tensor, HL[:, ds(m, 1), :], GA[0][:, :].unsqueeze(1),
                                  HH[:, ds(m, 1), :].bitcast(F32), ALU.subtract)
                        c_GA.set(tv)
                        hid.set(tv)

                    def c_of(c):
                        return half[0]

                    half = [0]
                    panel_epilogue(nk, (XH, XL), ready, ctx, gate_up, half)
                    t_hid = hid.t

                    def ready_h(k, nk=nk, t_hid=t_hid):
                        return t_hid if k == nk - 1 else [Ticket(V.sem, t_hid[0].c - per_chunk(ctx))]

                    gemm(NC // 2, nk, (HH, HL), ready_h, ctx, lambda c, j, t, g=g: down(c, g, j, t),
                         final=final and g == len(GROUPS) - 1)
                return everyone()

        def per_chunk(ctx):
            return 3 if ctx else 2

        def panel_epilogue(nk, rhs, ready, ctx, gate_up, half):
            pairs = nk // 2

            def body(i):
                for u in range(2):
                    half[0] = i * 2 + u
                    panel(u, NC, rhs, ready, ctx, gate_up, 0, False)
            book.repeat(pairs, body)
            split_n[0] += nk

        def add_to_x(l, g_col, ctx):
            def down(c, g, j, t):
                V.wait(t)
                V.take(c_X)
                for a, b, q in spans(ctx):
                    t = V.do(ve.scalar_tensor_tensor, X[:, ds(c, 1), a:b], PS[:, ds(2 * q + j, 1), 0:b - a],
                             mod[:, l, ds(c + g_col, 1), q:q + 1].rearrange("p a b -> p (a b)"),
                             X[:, ds(c, 1), a:b], ALU.mult, ALU.add)
                    bank[2 * q + j].set(t)
                c_X.set(t)
            return down

        def head_norm(dst, src, N, gain, src_t):
            A.wait(*src_t)
            A.take(c_SQ[0])
            t = A.do(ac.activation, SQ[0][:, 0:N], src, ACT.Square)
            T.wait(t)
            T.take(bank[6])
            T.take(bank[7])
            for a in range(0, N, BANK):
                b = min(N, a + BANK)
                t = T.do(te.matmul, PS[:, 6 + a // BANK, 0:b - a], BO, SQ[0][:, a:b], start=True, stop=True)
            c_SQ[0].set(t)
            inverse_root(6, N, t)
            V.take(c_RS)
            t = V.do(ve.scalar_tensor_tensor, dst, src, gain, RS[:, 0:N], ALU.mult, ALU.mult)
            c_RS.add(t)
            return t

        def rope(dst, src, N, tab, direct, rotate, t_src, t_dst):
            cos, sin = tab
            T.wait(*t_src)
            T.take(bank[6])
            T.take(bank[7])
            for a in range(0, N, BANK):
                b = min(N, a + BANK)
                t = T.do(te.matmul, PS[:, 6 + a // BANK, 0:b - a], rotate, src[:, a:b], start=True, stop=True)
            rot = PS[:, 6:8, :].rearrange("p b n -> p (b n)")
            V.wait(t, *t_dst)
            t = V.do(ve.tensor_tensor, dst, rot[:, 0:N], sin[:, 0:N], ALU.mult)
            if direct is not None:
                T.wait(t)
                for a in range(0, N, BANK):
                    b = min(N, a + BANK)
                    td = T.do(te.matmul, PS[:, 6 + a // BANK, 0:b - a], direct, src[:, a:b], start=True, stop=True)
                V.wait(td)
            plain = src if direct is None else rot[:, 0:N]
            V.take(c_SQ[1])
            V.wait(*t_src)
            t2 = V.do(ve.tensor_tensor, SQ[1][:, 0:N], plain, cos[:, 0:N], ALU.mult)
            bank[6].set(t2)
            bank[7].set(t2)
            V.wait(t2)
            t = V.do(ve.tensor_tensor, dst, dst, SQ[1][:, 0:N], ALU.add)
            c_SQ[1].set(t)
            return t

        def attend(scope, tag, dest, n_chunks, prep, tiles, K, Vt, groups, t_kv, t_mask, mask):
            QR = sb(f"QR_{tag}", [P, TOK], F32, scope)
            PB = [sb(f"PB{s}_{tag}", [P, TOK], F32, scope) for s in range(2)]
            PT = [sb(f"PT{s}_{tag}", [P, TOK], F32, scope) for s in range(2)]
            OT = [sb(f"OT{s}_{tag}", [P, P], F32, scope) for s in range(2)]
            nmax = [sb(f"nmax{s}_{tag}", [P, 1], F32, scope) for s in range(2)]
            rsum = [sb(f"rsum{s}_{tag}", [P, 1], F32, scope) for s in range(2)]
            c_QR, c_U = Carry(book), Carry(book)
            c_PB, c_PT, c_OT = ([Carry(book), Carry(book)] for _ in range(3))
            c_nm, c_rs = ([Carry(book), Carry(book)] for _ in range(2))
            steps = [(q0, k0, nk, dm, h) for q0, k0, nk, dm in tiles for h in range(2)]

            for grp in range(groups):
                kv_of = (lambda c: grp) if groups > 1 else (lambda c: c)

                def body(i, grp=grp):
                    c = i + grp * (n_chunks // groups)
                    V.take(c_QR)
                    A.take(c_QR)
                    t_q = prep(QR, c)
                    c_QR.set(t_q)

                    def scores(x):
                        q0, k0, nk, dm, h = steps[x]
                        b = x % 2
                        T.wait(t_q, *t_kv)
                        T.take(bank[2 * b])
                        T.take(bank[2 * b + 1])
                        hp = slice(h * HD, (h + 1) * HD)
                        for a in range(0, nk, BANK):
                            n = min(BANK, nk - a)
                            t = T.do(te.matmul, PS[:, 2 * b + a // BANK, 0:n], QR[hp, q0:q0 + P],
                                     K(hp, kv_of(c), k0 + a, n), start=True, stop=True)
                        c_QR.add(t)
                        S = PS[:, 2 * b:2 * b + 2, :].rearrange("p b n -> p (b n)")[:, 0:nk]
                        V.wait(t)
                        if dm:
                            V.wait(t_mask)
                            t = V.do(ve.tensor_tensor, S[:, nk - P:nk], S[:, nk - P:nk], mask, ALU.add)
                            V.wait(t)
                        V.take(c_nm[b])
                        t = V.do(ve.tensor_reduce, nmax[b][:], S, AX_X, ALU.max)
                        V.wait(t)
                        t = V.do(ve.tensor_scalar, nmax[b][:], nmax[b][:], -SCALE, None, ALU.mult)
                        A.wait(t)
                        A.take(c_PB[b])
                        A.take(c_rs[b])
                        t = A.do(ac.activation, PB[b][:, 0:nk], S, ACT.Exp, bias=nmax[b][:], scale=SCALE,
                                 accum_out=rsum[b][:])
                        c_nm[b].set(t)
                        bank[2 * b].set(t)
                        bank[2 * b + 1].set(t)
                        return t

                    def values(x, t_exp):
                        q0, k0, nk, dm, h = steps[x]
                        b, nkt = x % 2, nk // P
                        T.wait(t_exp)
                        T.take(bank[4])
                        T.take(bank[5])
                        low = nkt // 2
                        for kt in range(nkt):
                            to = PS[:, 4, kt * P:(kt + 1) * P] if kt < low else \
                                PS[:, 5, (kt - low) * P:(kt - low + 1) * P]
                            t = T.do(te.transpose, to, PB[b][:, kt * P:(kt + 1) * P], EYE,
                                     inc=kt in (low - 1, nkt - 1))
                            if kt == nkt // 2 - 1:
                                t_half = t
                        c_PB[b].set(t)
                        half = nkt // 2 * P
                        if half:
                            A.wait(t_half)
                            A.take(c_PT[b])
                            ta = A.do(ac.activation, PT[b][:, 0:half], PS[:, 4, 0:half], ACT.Copy)
                        V.wait(t)
                        V.take(c_PT[b])
                        tv = V.do(ve.tensor_copy, PT[b][:, half:nk], PS[:, 5, 0:nk - half])
                        bank[4].set(tv, *([ta] if half else []))
                        bank[5].set(tv, *([ta] if half else []))
                        V.wait(t_exp)
                        tr = V.do(ve.reciprocal, rsum[b][:], rsum[b][:])
                        T.wait(tv, *([ta] if half else []))
                        T.take(bank[6])
                        for kt in range(nkt):
                            t = T.do(te.matmul, PS[:, 6, 0:HD], PT[b][:, kt * P:(kt + 1) * P],
                                     Vt(kv_of(c), h, k0 // P + kt), start=kt == 0, stop=kt == nkt - 1,
                                     inc=kt == nkt - 1)
                        c_PT[b].set(t)
                        ob = (x // 2) % 2
                        V.wait(t, tr)
                        if h == 0:
                            V.take(c_OT[ob])
                        t = V.do(ve.tensor_scalar, OT[ob][:, h * HD:(h + 1) * HD], PS[:, 6, 0:HD], rsum[b][:], None,
                                 ALU.mult)
                        c_rs[b].set(t)
                        bank[6].set(t)
                        if h == 1:
                            T.wait(t)
                            T.take(bank[7])
                            t = T.do(te.transpose, PS[:, 7, 0:P], OT[ob][:, :], EYE)
                            c_OT[ob].set(t)
                            A.wait(t)
                            t = A.do(ac.activation, dest(c, q0), PS[:, 7, 0:P].unsqueeze(1), ACT.Copy)
                            bank[7].set(t)
                            c_U.set(t)

                    t_exp = scores(0)
                    for x in range(len(steps)):
                        nxt = scores(x + 1) if x + 1 < len(steps) else None
                        values(x, t_exp)
                        t_exp = nxt
                book.repeat(n_chunks // groups, body)

        def token_major(dst, src, n, t_src, t_dst):
            T.wait(*t_src)
            A.wait(*t_dst)
            for j in range(n):
                b = 4 + j % 2
                T.take(bank[b])
                t = T.do(te.transpose, PS[:, b, 0:P], src(j), EYE)
                A.wait(t)
                t = A.do(ac.activation, dst(j), PS[:, b, 0:P], ACT.Copy)
                bank[b].set(t)
            return t

        def fourier(l, U, ctx, t_in):
            with ExitStack() as scope:
                AB = sb(f"AB_{l}", [P, TOK // P, 2, 2, P], F32, scope)
                WF = sb(f"WF_{l}", [P, 2, 2 * P], F32, scope)
                Z = sb(f"Z_{l}", [P, 2, SEQ], F32, scope)
                FX = sb(f"FX_{l}", [P, 2, SEQ // P, SEQ], F32, scope)
                FC = sb(f"FC_{l}", [P, 2, CTX // P, CTX], F32, scope)
                G.wait(*t_in)
                t_tab = load(G, (WF[:], w_four[l]), (FX[:], dft_x), (FC[:], dft_c))
                T.wait(*t_in)
                A.wait(*t_in)
                V.wait(*t_in)
                T.wait(t_tab)
                t_ab = None
                for tt in range((TOK if ctx else SEQ) // P):
                    b = 4 + tt % 2
                    T.take(bank[b])
                    for fc in range(2):
                        for cs, W in enumerate((DC, DS)):
                            t = T.do(te.matmul, PS[:, b, (2 * fc + cs) * P:(2 * fc + cs + 1) * P],
                                     U[:, UF + fc, tt * P:(tt + 1) * P], W, start=True, stop=True)
                    A.wait(t)
                    t_ab = A.do(ac.activation, AB[:, tt].rearrange("p a b n -> p (a b n)"), PS[:, b, :], ACT.Copy)
                    bank[b].set(t_ab)
                for a, n, tab in ((0, SEQ, FX), (SEQ, CTX, FC))[:2 if ctx else 1]:
                    nt = n // P
                    T.wait(t_ab)
                    for fc in range(2):
                        T.take(bank[fc])
                        for x in range(2 * nt):
                            t = T.do(te.matmul, PS[:, fc, 0:n], AB[:, a // P + x // 2, fc, x % 2, :],
                                     tab[:, x % 2, x // 2, :], start=x == 0, stop=x == 2 * nt - 1)
                        V.wait(t)
                        tz = V.do(ve.tensor_copy, Z[:, fc, 0:n], PS[:, fc, 0:n])
                        bank[fc].set(tz)
                    T.wait(tz)
                    for m in range(2):
                        T.take(bank[2 + m])
                        for fc in range(2):
                            t = T.do(te.matmul, PS[:, 2 + m, 0:n], WF[:, fc, m * P:(m + 1) * P], Z[:, fc, 0:n],
                                     start=fc == 0, stop=fc == 1)
                        V.wait(t)
                        tz = V.do(ve.tensor_copy, U[:, UF + m, a:a + n], PS[:, 2 + m, 0:n])
                        bank[2 + m].set(tz)
                    V.wait(t)
            return everyone()

        def attention1(l, U, ctx, t_in):
            with ExitStack() as scope:
                tab = sb(f"rope_{l}", [P, 2, TOK], F32, scope)
                KK = sb(f"KK_{l}", [P, 2, TOK], F32, scope)
                VT = sb(f"VT_{l}", [P, TOK // P, P], F32, scope)
                qn = sb(f"qn_{l}", [P, TOK], F32, scope)
                for e in (T, A, V, G):
                    e.wait(*t_in)
                t_tab = load(G, (tab[:], rope1))
                T.wait(t_tab)
                V.wait(t_tab)
                cs = (tab[:, 0, :], tab[:, 1, :])
                t_k = head_norm(qn[:], U[:, UK, :], TOK, col("k_norm", l), [])
                for kv, (direct, rotate) in enumerate(((D0, R0), (D1, R1))):
                    t_kk = rope(KK[:, kv, :], qn[:, :], TOK, cs, direct, rotate, [t_k], [])
                t_v = token_major(lambda j: VT[:, j, :], lambda j: U[:, UV, j * P:(j + 1) * P], TOK // P, [], [])
                c_qn = Carry(book)
                c_qn.set(t_kk)
                N = TOK if ctx else SEQ

                def prep(QR, c):
                    V.take(c_qn)
                    src = U[:, ds(c + UQ, 1), 0:N].rearrange("p a n -> p (a n)")
                    t = head_norm(qn[:, 0:N], src, N, col("q_norm", l), [])
                    t = rope(QR[:, 0:N], qn[:, 0:N], N, cs, None, RQ, [t], [])
                    c_qn.set(t)
                    return t

                tiles = [(q, 0, TOK, False) for q in range(0, SEQ, P)]
                if ctx:
                    tiles += [(q, SEQ, CTX, False) for q in range(SEQ, TOK, P)]
                attend(scope, f"a{l}", lambda c, q0: U[:, ds(c + UQ, 1), q0:q0 + P], 4, prep, tiles,
                       lambda hp, kv, k0, n: KK[hp, kv, k0:k0 + n],
                       lambda kv, h, kt: VT[:, kt, kv * HD:(kv + 1) * HD], 2, [t_kk, t_v], None, None)
            return everyone()

        def hgrn(l, U, ctx, t_in):
            NT = TOK // P
            with ExitStack() as scope:
                cum = sb(f"cum_{l}", [P, 2, 2, TOK], F32, scope)
                E = [sb(f"E{d}_{l}", [P, LEVELS + 2, 2, P], F32, scope) for d in range(2)]
                VT = sb(f"hVT_{l}", [P, NT, 2 * P], F32, scope)
                VS = [sb(f"VS{d}_{l}", [P, 2 * P], F32, scope) for d in range(2)]
                KT = [sb(f"KT{d}_{l}", [P, 2 * P], F32, scope) for d in range(2)]
                att = [sb(f"att{d}_{l}", [P, 2, 2, P], F32, scope) for d in range(2)]
                MK = sb(f"MK_{l}", [P, 2, LEVELS, P], U32, scope)
                S = [sb(f"S{d}_{l}", [P, 2, P], F32, scope) for d in range(2)]
                el = [sb(f"el{d}_{l}", [P, 2], F32, scope) for d in range(2)]
                lb = sb(f"lb_{l}", [P, 2, 2], F32, scope)
                oml = sb(f"oml_{l}", [P, 2, 2], F32, scope)
                O = sb(f"O_{l}", [P, 2, TOK], F32, scope)
                for e in (T, A, V, G):
                    e.wait(*t_in)
                t_mk = load(G, (MK[:], masks))
                t_v = token_major(lambda j: VT[:, j // 2, (j % 2) * P:(j % 2 + 1) * P],
                                  lambda j: U[:, UI + j % 2, (j // 2) * P:(j // 2 + 1) * P], 2 * NT, [], [])
                if l == 0:
                    t_lb = V.do(ve.memset, lb[:], 0.0)
                else:
                    d01 = C[:, ds(COL["lb"], 8)].rearrange("p (d l f) -> p d l f", d=2, l=2)
                    t = V.do(ve.tensor_tensor, lb[:], d01[:, :, 1, :], d01[:, :, 0, :], ALU.subtract)
                    A.wait(t)
                    t_lb = A.do(ac.activation, lb[:], lb[:], ACT.Sigmoid)
                V.wait(t_lb)
                t_lb = V.do(ve.tensor_scalar, oml[:], lb[:], -1.0, 1.0, ALU.mult, ALU.add)
                t_f = []
                for d in range(2):
                    for fc in range(2):
                        z = U[:, UFF + 2 * d + fc, :]
                        Et = E[d][:].rearrange("p a b n -> p (a b n)")[:, fc * TOK:(fc + 1) * TOK]
                        t = A.do(ac.activation, Et, z, ACT.Sigmoid)
                        A.wait(t)
                        t2 = A.do(ac.activation, z, z, ACT.Sigmoid, scale=-1.0)
                        V.wait(t, t_lb)
                        t = V.do(ve.tensor_scalar, Et, Et, oml[:, d, fc:fc + 1], lb[:, d, fc:fc + 1],
                                 ALU.mult, ALU.add)
                        V.wait(t)
                        t = V.do(ve.tensor_scalar, Et, Et, 2.0 ** -63, None, ALU.max)
                        t_f.append(t)
                        V.wait(t2)
                        t_k = V.do(ve.tensor_scalar, z, z, oml[:, d, fc:fc + 1], None, ALU.mult)
                tm = V.do(ve.memset, SQ[0][:], 1.0)
                V.wait(tm)
                tm = V.do(ve.memset, SQ[0][:].rearrange("p (j t) -> p j t", t=P)[:, :, 0:1], 0.0)
                V.wait(tm)
                tm = V.do(ve.memset, SQ[1][:], 1.0)
                V.wait(tm)
                tm = V.do(ve.memset, SQ[1][:].rearrange("p (j t) -> p j t", t=P)[:, :, P - 1:P], 0.0)
                V.wait(tm)
                for d in range(2):
                    for fc in range(2):
                        Et = E[d][:].rearrange("p a b n -> p (a b n)")[:, fc * TOK:(fc + 1) * TOK]
                        A.wait(t_f[2 * d + fc])
                        t = A.do(ac.activation, Et, Et, ACT.Ln)
                        V.wait(t)
                        st = 1 if d == 0 else -1
                        t_cum = V.do(ve.tensor_tensor_scan, cum[:, d, fc, ::st], SQ[d][:, ::st], Et[:, ::st], 0.0,
                                     ALU.mult, ALU.add)
                c_SQ[0].set(t_cum)
                c_SQ[1].set(t_cum)
                N = TOK if ctx else SEQ
                V.wait(t_k)
                for fc in range(2):
                    t = V.do(ve.tensor_tensor, O[:, fc, 0:N], U[:, UFF + fc, 0:N], U[:, UFB + fc, 0:N], ALU.add)
                    V.wait(t)
                    t = V.do(ve.tensor_tensor, O[:, fc, 0:N], O[:, fc, 0:N], U[:, UHQ + fc, 0:N], ALU.mult)
                    T.wait(t)
                    T.take(bank[6])
                    T.take(bank[7])
                    for a in range(0, N, BANK):
                        b = min(N, a + BANK)
                        t = T.do(te.matmul, PS[:, 6 + a // BANK, 0:b - a], BO, O[:, fc, a:b], start=True, stop=True)
                    V.wait(t)
                    t_o = V.do(ve.scalar_tensor_tensor, O[:, fc, 0:N],
                               PS[:, 6:8, :].rearrange("p b n -> p (b n)")[:, 0:N], float(HD), U[:, UI + fc, 0:N],
                               ALU.mult, ALU.mult)
                    bank[6].set(t_o)
                    bank[7].set(t_o)
                c_O, c_S = Carry(book), [Carry(book), Carry(book)]
                c_O.set(t_o)
                c_E, c_att, c_VS, c_KT, c_el = ([Carry(book), Carry(book)] for _ in range(5))
                for d in range(2):
                    t = V.do(ve.memset, att[d][:], 0.0)
                    c_att[d].set(t)
                    t = V.do(ve.memset, S[d][:], 0.0)
                    c_S[d].set(t)
                    c_E[d].set(t_cum)
                for e in (T, A, V, G):
                    e.wait(t_mk, t_cum, t_k, t_v, t_o, t)

                def halves(ap, h):
                    return ap.rearrange("p f (b t) -> p f b t", t=2 * h)

                def step(d, j, with_out):
                    tok = ds(j * P, P)
                    cu = cum[:, d, :, tok]
                    q, k, Ed = U[:, UHQ:UHQ + 2, tok], U[:, UFF + 2 * d:UFF + 2 * d + 2, tok], E[d]
                    V.take(c_E[d])
                    A.take(c_E[d])
                    edge = P - 1 if d == 0 else 0
                    if with_out:
                        for lv in range(LEVELS):
                            h = P >> (lv + 1)
                            src, dst = halves(cu, h), halves(Ed[:, lv], h)
                            mid = h - 1 if d == 0 else h
                            ref = src[:, :, :, mid:mid + 1].broadcast_to([P, 2, P // (2 * h), h])
                            late = slice(h, 2 * h) if d == 0 else slice(0, h)
                            early = slice(0, h) if d == 0 else slice(h, 2 * h)
                            V.do(ve.tensor_tensor, dst[:, :, :, late], src[:, :, :, late], ref, ALU.subtract)
                            t = V.do(ve.tensor_tensor, dst[:, :, :, early], ref, src[:, :, :, early], ALU.subtract)
                    t = V.do(ve.tensor_tensor, Ed[:, LEVELS + 1], cu[:, :, edge:edge + 1].broadcast_to([P, 2, P]), cu,
                             ALU.subtract)
                    A.take(c_el[d])
                    t_el = A.do(ac.activation, el[d][:], cu[:, :, edge], ACT.Exp)
                    A.take(c_VS[d])
                    t_vs = A.do(ac.activation, VS[d][:].unsqueeze(1), VT[:, ds(j, 1), :], ACT.Copy)
                    if with_out:
                        t_l7 = A.do(ac.activation, Ed[:, LEVELS], cu, ACT.Exp)
                    A.wait(t)
                    t_x = A.do(ac.activation, Ed[:, LEVELS + 1], Ed[:, LEVELS + 1], ACT.Exp)
                    G.wait(t_x)
                    t_kd = G.do(gp.tensor_tensor, Ed[:, LEVELS + 1], Ed[:, LEVELS + 1], k, ALU.mult)
                    if with_out:
                        lv_t = []
                        t_x = A.do(ac.activation, Ed[:, 0:LEVELS], Ed[:, 0:LEVELS], ACT.Exp)
                        G.wait(t_x)
                        V.wait(t_x)
                        for lv in range(LEVELS):
                            h = P >> (lv + 1)
                            W, qq, kk = halves(Ed[:, lv], h), halves(q, h), halves(k, h)
                            late = slice(h, 2 * h) if d == 0 else slice(0, h)
                            early = slice(0, h) if d == 0 else slice(h, 2 * h)
                            eng, op = ((V, ve.tensor_tensor), (G, gp.tensor_tensor))[lv % 2]
                            eng.do(op, W[:, :, :, late], W[:, :, :, late], qq[:, :, :, late], ALU.mult)
                            lv_t.append(eng.do(op, W[:, :, :, early], W[:, :, :, early], kk[:, :, :, early],
                                               ALU.mult))
                        t_l7 = V.do(ve.tensor_tensor, Ed[:, LEVELS], Ed[:, LEVELS], q, ALU.mult)
                        V.take(c_att[d])
                        for lv in range(LEVELS):
                            T.wait(lv_t[lv])
                            T.take(bank[2 * d])
                            for hh in (0, 2, 1, 3):
                                hp = slice((hh % 2) * HD, (hh % 2 + 1) * HD)
                                w = Ed[hp, lv, hh // 2, :]
                                t = T.do(te.matmul, PS[:, 2 * d + hh % 2, (hh // 2) * P:(hh // 2 + 1) * P], w, w,
                                         start=True, stop=True, inc=hh == 3)
                            V.wait(t)
                            t_at = V.do(ve.copy_predicated, att[d][:],
                                        MK[:, d, lv, :].unsqueeze(1).unsqueeze(1).broadcast_to([P, 2, 2, P]),
                                        PS[:, 2 * d:2 * d + 2, 0:2 * P].rearrange("p a (b n) -> p a b n", b=2))
                            bank[2 * d].set(t_at)
                            bank[2 * d + 1].set(t_at)
                        T.wait(t_at, t_vs, t_l7)
                        T.take(c_S[d])
                        T.take(bank[6 + d])
                        for fc in range(2):
                            T.do(te.matmul, PS[:, 6 + d, fc * P:(fc + 1) * P], S[d][:, fc, :], Ed[:, LEVELS, fc, :],
                                 start=True, stop=False, inc=False, skip_group_check=True)
                            for hf in range(2):
                                hp = slice(hf * HD, (hf + 1) * HD)
                                t = T.do(te.matmul, PS[hp, 6 + d, fc * P:(fc + 1) * P],
                                         VS[d][:, fc * P + hf * HD:fc * P + (hf + 1) * HD], att[d][:, hf, fc, :],
                                         start=False, stop=True, skip_group_check=True)
                        c_att[d].set(t)
                        c_S[d].add(t)
                        V.wait(t)
                        V.take(c_O)
                        ot = O[:, :, tok]
                        t = V.do(ve.tensor_tensor, ot, PS[:, 6 + d, 0:2 * P].rearrange("p (f n) -> p f n", f=2), ot,
                                 ALU.add)
                        bank[6 + d].set(t)
                        c_O.set(t)
                    T.wait(t_kd, t_vs)
                    T.take(bank[4 + d])
                    for fc in range(2):
                        t = T.do(te.transpose, PS[:, 4 + d, fc * P:(fc + 1) * P], Ed[:, LEVELS + 1, fc, :], EYE)
                    c_E[d].set(t)
                    A.wait(t)
                    A.take(c_KT[d])
                    t = A.do(ac.activation, KT[d][:], PS[:, 4 + d, 0:2 * P], ACT.Copy)
                    T.wait(t)
                    for fc in range(2):
                        t = T.do(te.matmul, PS[:, 4 + d, 2 * P + fc * P:2 * P + (fc + 1) * P],
                                 KT[d][:, fc * P:(fc + 1) * P], VS[d][:, fc * P:(fc + 1) * P], start=True, stop=True)
                    c_KT[d].set(t)
                    c_VS[d].set(t)
                    V.wait(t, t_el)
                    V.take(c_S[d])
                    for fc in range(2):
                        for hf in range(2):
                            hp = slice(hf * HD, (hf + 1) * HD)
                            t = V.do(ve.scalar_tensor_tensor, S[d][hp, fc, hf * HD:(hf + 1) * HD],
                                     S[d][hp, fc, hf * HD:(hf + 1) * HD], el[d][hp, fc:fc + 1],
                                     PS[hp, 4 + d, 2 * P + fc * P + hf * HD:2 * P + fc * P + (hf + 1) * HD],
                                     ALU.mult, ALU.add)
                    c_S[d].set(t)
                    c_el[d].set(t)
                    bank[4 + d].set(t)

                nx, nctx = SEQ // P, CTX // P

                def ctx_body(i):
                    step(0, i + nx, ctx)
                    step(1, i * -1 + (NT - 1), ctx)

                def x_body(i):
                    step(0, i, True)
                    step(1, i * -1 + (nx - 1), True)
                book.repeat(nctx, ctx_body)
                book.repeat(nx, x_body)
                A.wait(*c_O.t)
                for fc in range(2):
                    t_g = A.do(ac.activation, U[:, UG + fc, 0:N], U[:, UG + fc, 0:N], ACT.Silu)
                    t = head_norm(O[:, fc, 0:N], O[:, fc, 0:N], N, col("hg_norm", l), c_O.t)
                    V.wait(t, t_g)
                    V.do(ve.tensor_tensor, U[:, 6 + fc, 0:N], O[:, fc, 0:N], U[:, UG + fc, 0:N], ALU.mult)
            return everyone()

        def checkpoint(name):
            if dbg is not None and name in dbg:
                sem = semaphore("dbg_" + name)
                t = everyone()
                G.wait(*t)
                G.flush()
                gp.dma_start(dbg[name], X[:, :, :]).then_inc(sem, 16)
                for e in (T, A, V, G):
                    e.wait(Ticket(sem, 16))
            return stop == name

        def finish(wait):
            for e in (T, V, G):
                e.flush()
            outs = semaphore("out_landed")
            A.wait(*wait)
            A.flush()
            ac.dma_start(out, X[:, :, 0:SEQ]).then_inc(outs, 16)
            ac.wait_ge(outs, 16)

        with ExitStack() as first:
            cv = sb("cv", [P, NC, 2], F32, first)
            t = load(A, (cv[:], cvec))
            A.wait(t)
            t_cv = A.do(ac.activation, cv[:], cv[:], ACT.Silu)
            A.wait(t_cv_x, t_const)
            V.wait(t_cv_x, t_const)
            T.wait(t_const)
            mean_square(lambda c: X[:, c, :], NC, True)
            modulation(0, cv, t_cv)
            split(0)
            for l in range(DEPTH):
                full = l < DEPTH - 1
                if l:
                    modulation(l, cv, t_cv)

                def gain_of(j, l=l):
                    return lambda c, q: mod[:, l, j + c, q:q + 1]

                with ExitStack() as mixing:
                    U = sb(f"U_{l}", [P, UN, TOK], F32, mixing)
                    with ExitStack() as scope:
                        XH = sb(f"XHp_{l}", [P, NC, TOK], F32R, scope)
                        XL = sb(f"XLp_{l}", [P, NC, TOK], F32R, scope)
                        free = everyone()
                        if l:
                            mean_square(lambda c: X[:, c, :], NC, True)
                        ready = normed(XH, XL, True, gain_of(SC_A), gain_of(SH_A), free)

                        def project(ctx):
                            def epilogue(c, j, t):
                                A.wait(t)
                                ta = A.do(ac.activation, U[:, ds(c, 1), 0:SEQ], PS[:, j:j + 1, 0:SEQ], ACT.Copy)
                                bank[j].set(ta)
                                if ctx:
                                    V.wait(t)
                                    tv = V.do(ve.tensor_copy, U[:, ds(c, 1), SEQ:TOK], PS[:, 2 + j:3 + j, 0:CTX])
                                    bank[2 + j].set(tv)
                            return epilogue
                        if full:
                            gemm(UN // 2, NC, (XH, XL), ready, True, project(True))
                        else:
                            gemm(UK // 2, NC, (XH, XL), ready, False, project(False))
                            gemm((UHQ - UK) // 2, NC, (XH, XL), ready, True, project(True), first=UK // 2)
                            gemm((UN - UHQ) // 2, NC, (XH, XL), ready, False, project(False), first=UHQ // 2)
                    t = fourier(l, U, full, everyone())
                    t = attention1(l, U, full, t)
                    t = hgrn(l, U, full, t)
                    with ExitStack() as scope:
                        N = TOK if full else SEQ
                        XH = sb(f"XHo_{l}", [P, NC, N], F32R, scope)
                        XL = sb(f"XLo_{l}", [P, NC, N], F32R, scope)
                        ready = split_chunks(XH, XL, lambda c: U[:, c, :], NC, full, t, t)
                        add = add_to_x(l, G_A, full)
                        gemm(NC // 2, NC, (XH, XL), ready, full, lambda c, j, t: add(c, 0, j, t))
                if checkpoint(f"mix{l}"):
                    finish(everyone())
                    return
                ffn(f"f{l}", full, gain_of(SC_F), gain_of(SH_F), add_to_x(l, G_F, full))
                if checkpoint(f"ffn{l}"):
                    finish(everyone())
                    return
            mean_square(lambda c: X[:, c, :], NC, False)
            V.take(c_RS)
            V.take(c_X)
            for c in range(NC):
                t = V.do(ve.scalar_tensor_tensor, X[:, c, 0:SEQ], X[:, c, 0:SEQ], col("final", c), RS[:, 0:SEQ],
                         ALU.mult, ALU.mult)
            c_RS.add(t)
            c_X.set(t)

        def post_norm(src, g, half, ready):
            A.wait(*ready)
            V.wait(*ready)
            mean_square(src, NC, False)
            V.take(c_RS)
            t = V.do(ve.tensor_scalar, col("post", g * NC, NC), col("post", g * NC, NC), 0.5 if half else 1.0, None,
                     ALU.mult)
            V.wait(t)
            V.take(c_X)
            for c in range(NC):
                u = c % 2
                V.take(c_SQ[u])
                t = V.do(ve.scalar_tensor_tensor, SQ[u][:, 0:SEQ], src(c)[:, 0:SEQ], col("post", g * NC + c),
                         RS[:, 0:SEQ], ALU.mult, ALU.mult)
                V.wait(t)
                t = V.do(ve.tensor_tensor, X[:, c, 0:SEQ], X[:, c, 0:SEQ], SQ[u][:, 0:SEQ], ALU.add)
                c_SQ[u].set(t)
            c_RS.add(t)
            c_X.set(t)

        def pre_gain(g):
            return lambda c, q: col("pre", g * NC + c)

        def store(dst, evict=True):
            def epilogue(c, j, t):
                A.wait(t)
                ta = A.do(ac.activation, dst(c), PS[:, j:j + 1, :], ACT.Copy)
                bank[j].set(ta)
            return epilogue

        def ffn2(tag, g, final=False):
            with ExitStack() as scope:
                Y = sb(f"Y_{tag}", [P, NC, SEQ], F32, scope)
                c_Y = Carry(book)
                c_Y.set(*everyone())

                def down(c, grp, j, t):
                    V.wait(t)
                    V.take(c_Y)
                    y = Y[:, ds(c, 1), :]
                    if grp == 0:
                        t = V.do(ve.tensor_copy, y, PS[:, j:j + 1, :])
                    else:
                        t = V.do(ve.tensor_tensor, y, PS[:, j:j + 1, :], y, ALU.add)
                    bank[j].set(t)
                    c_Y.set(t)
                ffn(tag, False, pre_gain(g), None, down, final)
                post_norm(lambda c: Y[:, c, :], g, True, c_Y.t)

        def attention2(U, t_in):
            with ExitStack() as scope:
                tab = sb("rope2_t", [P, 2, SEQ], F32, scope)
                cm = sb("cm", [P, P], F32, scope)
                KR = sb("KR2", [P, SEQ], F32, scope)
                VT = sb("VT2", [P, SEQ // P, 4 * P], F32, scope)
                for e in (T, A, V, G):
                    e.wait(*t_in)
                t_tab = load(G, (tab[:], rope2), (cm[:], causal))
                V.wait(t_tab)
                cs = (tab[:, 0, :], tab[:, 1, :])
                t_v = token_major(lambda j: VT[:, j // 4, (j % 4) * P:(j % 4 + 1) * P],
                                  lambda j: U[:, 8 + j % 4, (j // 4) * P:(j // 4 + 1) * P], 4 * (SEQ // P), [], [])

                def prep(QR, c):
                    rope(KR[:], U[:, ds(c + 4, 1), :].rearrange("p a n -> p (a n)"), SEQ, cs, None, R2, [], [])
                    return rope(QR[:, 0:SEQ], U[:, ds(c, 1), :].rearrange("p a n -> p (a n)"), SEQ, cs, None, R2,
                                [], [])
                tiles = [(q, 0, q + P, True) for q in range(0, SEQ, P)]
                attend(scope, "m", lambda c, q0: U[:, ds(c, 1), q0:q0 + P], 4, prep, tiles,
                       lambda hp, kv, k0, n: KR[hp, k0:k0 + n],
                       lambda kv, h, kt: VT[:, kt, ds(kv * P + h * HD, HD)], 1, [t_v], t_tab, cm[:])
            return everyone()

        def lru(U, t_in):
            with ExitStack() as scope:
                WG = sb("WG", [P, 2, 4, P], F32, scope)
                xc = [sb(f"xc{s}", [P, SEQ], F32, scope) for s in range(2)]
                r_, i_, u_, a_ = ([sb(f"lru_{n}{s}", [P, SEQ], F32, scope) for s in range(2)] for n in "riua")
                sp_ = sb("sp_", [P, 4], F32, scope)
                sq_ = sb("sq_", [P, 4], F32, scope)
                for e in (T, A, V, G):
                    e.wait(*t_in)
                t_w = load(G, (WG[:], lru_gates))
                t = A.do(ac.activation, sp_[:], col("lam", 0, 4), ACT.Abs)
                A.wait(t)
                t = A.do(ac.activation, sp_[:], sp_[:], ACT.Exp, scale=-1.0)
                V.wait(t)
                t = V.do(ve.tensor_scalar, sp_[:], sp_[:], 1.0, None, ALU.add)
                A.wait(t)
                t = A.do(ac.activation, sp_[:], sp_[:], ACT.Ln)
                t2 = V.do(ve.tensor_scalar, sq_[:], col("lam", 0, 4), -1.0, 0.0, ALU.mult, ALU.max)
                V.wait(t, t2)
                t = V.do(ve.tensor_tensor, sp_[:], sp_[:], sq_[:], ALU.add)
                V.wait(t)
                t_sp = V.do(ve.tensor_scalar, sp_[:], sp_[:], -8.0, None, ALU.mult)
                c_u = [Carry(book), Carry(book)]
                for c in range(4):
                    s = c % 2
                    V.take(c_u[s])
                    A.take(c_u[s])
                    src, x = U[:, 12 + c, :], xc[s]
                    t = V.do(ve.tensor_scalar, x[:], src, col("conv_w", 3 * 4 + c), col("conv_b", c),
                             ALU.mult, ALU.add)
                    for back in range(1, 4):
                        V.wait(t)
                        t = V.do(ve.scalar_tensor_tensor, x[:, back:SEQ], src[:, 0:SEQ - back],
                                 col("conv_w", (3 - back) * 4 + c), x[:, back:SEQ], ALU.mult, ALU.add)
                    V.wait(t)
                    T.wait(t, t_w)
                    ts = []
                    for g, (dst, b) in enumerate(((r_[s], "ba"), (i_[s], "bx"))):
                        T.take(bank[2 * s + g])
                        t = T.do(te.matmul, PS[:, 2 * s + g, :], WG[:, g, c, :], x[:], start=True, stop=True)
                        A.wait(t)
                        t = A.do(ac.activation, dst[:], PS[:, 2 * s + g, :], ACT.Sigmoid, bias=col(b, c))
                        bank[2 * s + g].set(t)
                        ts.append(t)
                    t_gelu = A.do(ac.activation, U[:, 16 + c, :], U[:, 16 + c, :], ACT.Gelu_apprx_tanh)
                    V.wait(ts[0], t_sp)
                    t = V.do(ve.tensor_scalar, r_[s][:], r_[s][:], sp_[:, c:c + 1], None, ALU.mult)
                    A.wait(t)
                    t_a = A.do(ac.activation, a_[s][:], r_[s][:], ACT.Exp)
                    t_t = A.do(ac.activation, u_[s][:], r_[s][:], ACT.Tanh, scale=-1.0)
                    V.wait(t_a, t_t, ts[1])
                    t1 = V.do(ve.tensor_tensor, r_[s][:], a_[s][:], a_[s][:], ALU.mult)
                    V.wait(t1)
                    t1 = V.do(ve.scalar_tensor_tensor, u_[s][:], r_[s][:], 1.0, u_[s][:], ALU.add, ALU.mult)
                    V.wait(t1)
                    t1 = V.do(ve.tensor_scalar, u_[s][:], u_[s][:], 1e-34, None, ALU.max)
                    t2 = V.do(ve.tensor_tensor, i_[s][:], i_[s][:], x[:], ALU.mult)
                    A.wait(t1)
                    t = A.do(ac.activation, u_[s][:], u_[s][:], ACT.Sqrt)
                    V.wait(t, t2)
                    t = V.do(ve.tensor_tensor, u_[s][:], u_[s][:], i_[s][:], ALU.mult)
                    V.wait(t)
                    t = V.do(ve.tensor_tensor_scan, r_[s][:], a_[s][:], u_[s][:], 0.0, ALU.mult, ALU.add)
                    V.wait(t, t_gelu)
                    t = V.do(ve.tensor_tensor, U[:, 4 + c, :], r_[s][:], U[:, 16 + c, :], ALU.mult)
                    c_u[s].set(t)
            return everyone()

        def short_conv(U, t_in):
            with ExitStack() as scope:
                y = [sb(f"y{s}", [P, SEQ], F32, scope) for s in range(2)]
                c_y = [Carry(book), Carry(book)]
                V.wait(*t_in)
                for c in range(NC):
                    s = c % 2
                    cx = U[:, 16 + c, :]
                    t = V.do(ve.tensor_tensor, cx, cx, U[:, 8 + c, :], ALU.mult)
                    V.wait(t)
                    V.take(c_y[s])
                    t = V.do(ve.tensor_scalar, y[s][:], cx, col("c_conv", 2 * NC + c), None, ALU.mult)
                    for back in range(1, 3):
                        V.wait(t)
                        t = V.do(ve.scalar_tensor_tensor, y[s][:, back:SEQ], cx[:, 0:SEQ - back],
                                 col("c_conv", (2 - back) * NC + c), y[s][:, back:SEQ], ALU.mult, ALU.add)
                    V.wait(t)
                    t = V.do(ve.tensor_tensor, U[:, c, :], U[:, c, :], y[s][:], ALU.mult)
                    c_y[s].set(t)
            return everyone()

        for l in range(DEPTH):
            ffn2(f"a{l}", 3 * l)
            if checkpoint(f"b{l}0"):
                finish(everyone())
                return
            n_in = (20, 24)[l]
            with ExitStack() as mixing:
                U = sb(f"U2_{l}", [P, n_in, SEQ], F32, mixing)
                with ExitStack() as scope:
                    XH = sb(f"XHq_{l}", [P, NC, SEQ], F32R, scope)
                    XL = sb(f"XLq_{l}", [P, NC, SEQ], F32R, scope)
                    free = everyone()
                    mean_square(lambda c: X[:, c, :], NC, False)
                    ready = normed(XH, XL, False, pre_gain(3 * l + 1), None, free)
                    gemm(n_in // 2, NC, (XH, XL), ready, False, store(lambda c: U[:, ds(c, 1), :]))
                if l == 0:
                    t = attention2(U, everyone())
                    t = lru(U, t)
                else:
                    t = short_conv(U, everyone())
                with ExitStack() as scope:
                    XH = sb(f"XHr_{l}", [P, NC, SEQ], F32R, scope)
                    XL = sb(f"XLr_{l}", [P, NC, SEQ], F32R, scope)
                    ready = split_chunks(XH, XL, lambda c: U[:, c, :], NC, False, t, t)
                    gemm(NC // 2, NC, (XH, XL), ready, False, store(lambda c: U[:, ds(c + 8, 1), :]))
                    post_norm(lambda c: U[:, 8 + c, :], 3 * l + 1, False, everyone())
            if checkpoint(f"b{l}1"):
                finish(everyone())
                return
            ffn2(f"b{l}", 3 * l + 2, final=l == DEPTH - 1)
            if checkpoint(f"b{l}2"):
                finish(everyone())
                return
        finish(everyone())


def rotation(pairs, heads=2, source=None):
    m = np.zeros((P, P), np.float32)
    for h in range(heads):
        base = (source if source is not None else h) * HD
        for first, w in pairs:
            for j in range(first, first + w):
                m[base + j + w, h * HD + j] = -1
                m[base + j, h * HD + j + w] = 1
    return m


def block_diagonal(a):
    m = np.zeros((P, P), np.float32)
    m[:HD, :HD] = m[HD:, HD:] = a
    return m


def tables():
    f = np.float32
    d = np.arange(HD)
    ang = 2 * np.pi * ((d[:, None] * d[None, :]) % HD) / HD
    axial = [(0, 16), (32, 16)]
    copy = [np.zeros((P, P), f) for _ in range(2)]
    for kv in range(2):
        for h in range(2):
            copy[kv][kv * HD + d, h * HD + d] = 1
    mats = np.stack([
        np.full((P, P), 1 / D, f), np.eye(P, dtype=f), block_diagonal(np.full((HD, HD), 1 / HD, f)),
        rotation(axial), copy[0], copy[1], rotation(axial, source=0), rotation(axial, source=1),
        rotation([(0, 8)]), block_diagonal(np.cos(ang) / 8), block_diagonal(np.sin(ang) / 8),
    ], 1).astype(f)

    def dft(n):
        a = 2 * np.pi * ((np.arange(n)[:, None] * np.arange(n)[None, :]) % n) / n
        t = np.stack([np.cos(a), -np.sin(a)]) / np.sqrt(n)
        return np.ascontiguousarray(t.reshape(2, n // P, P, n).transpose(2, 0, 1, 3)).astype(f)

    freqs = (f(10000.0) ** (-np.arange(0, 32, 2, dtype=f) / f(32))).astype(f)
    pos = np.arange(SEQ)
    ar = ((pos // 64).astype(f)[:, None] * freqs).T
    ak = ((pos % 64).astype(f)[:, None] * freqs).T
    angles = np.concatenate([ar, ar, ak, ak] * 2, 0)
    rope1 = np.zeros((P, 2, TOK), f)
    rope1[:, 0] = 1
    rope1[:, 0, :SEQ], rope1[:, 1, :SEQ] = np.cos(angles), np.sin(angles)
    inv = (f(500000.0) ** (-np.arange(0, 16, 2, dtype=f) / f(16))).astype(f)
    a2 = (pos.astype(f)[:, None] * inv).T
    rope2 = np.zeros((P, 2, SEQ), f)
    rope2[:, 0] = 1
    for h in range(2):
        for part in range(2):
            rope2[h * HD + part * 8:h * HD + part * 8 + 8, 0] = np.cos(a2)
            rope2[h * HD + part * 8:h * HD + part * 8 + 8, 1] = np.sin(a2)
    masks = np.zeros((P, 2, LEVELS, P), np.uint32)
    s, t = np.arange(P)[:, None], np.arange(P)[None, :]
    for lv in range(LEVELS):
        h = P >> (lv + 1)
        same = s // (2 * h) == t // (2 * h)
        masks[:, 0, lv] = same & (s % (2 * h) < h) & (t % (2 * h) >= h)
        masks[:, 1, lv] = same & (s % (2 * h) >= h) & (t % (2 * h) < h)
    causal = np.where(np.arange(P)[None, :] <= np.arange(P)[:, None], 0, NEG).astype(f)
    return dict(mats=mats, rope1=rope1, rope2=rope2, dft_x=dft(SEQ), dft_c=dft(CTX), masks=masks, causal=causal)


def chunks(v):
    v = np.asarray(v)
    v = v.reshape(v.shape[:-1] + (v.shape[-1] // P, P))
    return np.moveaxis(v, -1, 0).reshape(P, -1)


def column_panels(w):
    k, n = w.shape
    w = w.reshape(k // P, P, n // 256, 256).transpose(2, 1, 0, 3)
    if k < D:
        w = np.concatenate([w, np.zeros((n // 256, P, (D - k) // P, 256), w.dtype)], 2)
    return w.reshape(n // 256, P, PANEL)


def ffn_panels(gate, up, down):
    both = np.concatenate([gate.reshape(D, DFF // P, P), up.reshape(D, DFF // P, P)], 2).reshape(D, 2 * DFF)
    both = column_panels(both)
    out, at = [], 0
    for nk in GROUPS:
        out += [both[at:at + nk], column_panels(down[at * P:(at + nk) * P])]
        at += nk
    return out


def lay_out(a):
    a = {k: np.asarray(v) for k, v in a.items()}
    x = np.concatenate([a["x"][0], a["ctx"][0]], 0)
    xT = np.ascontiguousarray(x.T.reshape(NC, P, TOK).transpose(1, 0, 2))
    cvec = np.ascontiguousarray(np.stack([chunks(a["c"][0]), chunks(a["c_ctx"])], 2))
    two = lambda v: np.concatenate([v, v], -1)
    cols = np.concatenate([
        chunks(a["b_ada"]), two(a["q_norm"]).T, two(a["k_norm"]).T, two(a["hg_norm"]).T, chunks(a["hg_lb_logits"]),
        chunks(a["final_norm"]), chunks(a["norm_pre_2"]), chunks(a["norm_post_2"]), chunks(a["lru_conv_w_2"][0]),
        chunks(a["lru_conv_b_2"][0]), chunks(a["lru_gate_a_b_2"].reshape(-1)),
        chunks(a["lru_gate_x_b_2"].reshape(-1)), chunks(a["lru_lambda_2"][0]), chunks(a["c_conv_w_2"][0]),
    ], 1)
    parts = []
    for l in range(DEPTH):
        parts += [column_panels(a["w_in"][l]), column_panels(a["w_out"][l])]
        parts += ffn_panels(a["w_gate"][l], a["w_up"][l], a["w_down"][l])
    for l in range(DEPTH):
        parts += ffn_panels(a["ffn1_w_gate_2"][l], a["ffn1_w_up_2"][l], a["ffn1_w_down_2"][l])
        w_in, w_out = (a["ab_w_in_2"][0], a["ab_w_out_2"][0]) if l == 0 else (a["c_w_in_2"][0], a["c_w_out_2"][0])
        parts += [column_panels(w_in), column_panels(w_out)]
        parts += ffn_panels(a["ffn2_w_gate_2"][l], a["ffn2_w_up_2"][l], a["ffn2_w_down_2"][l])
    panels = np.concatenate(parts, 0)
    assert len(panels) % 2 == 0, len(panels)
    ada = np.concatenate([column_panels(a["w_ada"][l]) for l in range(DEPTH)], 0)
    w_four = np.ascontiguousarray(a["w_four"].reshape(DEPTH, 2, P, 2 * P).transpose(0, 2, 1, 3))
    gates = np.zeros((P, 2, 4, P), np.float32)
    for g, w in enumerate((a["lru_gate_a_w_2"][0], a["lru_gate_x_w_2"][0])):
        for h in range(8):
            r = slice((h % 2) * HD, (h % 2 + 1) * HD)
            gates[r, g, h // 2, r] = w[h]
    return dict(xT=xT, cvec=cvec, cols=np.ascontiguousarray(cols), panels=panels, ada_panels=ada, w_four=w_four,
                lru_gates=gates, **tables())


def kernel(**inputs):
    import concourse.bacc as bacc
    from concourse.bass_utils import run_bass_kernel_spmd

    arrays = lay_out(inputs)
    nc = bacc.Bacc("TRN2", target_bir_lowering=False, num_devices=1)
    args = {n: nc.dram_tensor(f"in_{n}", v.shape, mybir.dt.from_np(v.dtype), kind="ExternalInput").ap()
            for n, v in arrays.items()}
    out = nc.dram_tensor("out_0", (P, NC, SEQ), F32, kind="ExternalOutput").ap()
    program(nc, out=out, **args)
    r = run_bass_kernel_spmd(nc, [{f"in_{n}": v for n, v in arrays.items()}], core_ids=[0])
    got = r.results[0]["out_0"]
    return got.transpose(2, 1, 0).reshape(1, SEQ, D)
```

```python
from contextlib import ExitStack

import numpy as np

import concourse.bass as bass
from concourse import mybir

F32 = mybir.dt.float32
F32R = mybir.dt.float32r
U8 = mybir.dt.uint8
ALU = mybir.AluOpType
ACT = mybir.ActivationFunctionType
AX_X = mybir.AxisListType.X

P = 128
D = 1024
NC = D // P
SEQ, CTX = 512, 256
TOK = SEQ + CTX
BANK = 512
DEPTH = 2
HD = 64
DFF = 2816
GROUPS = [8, 8, 6]
PANEL = NC * 2 * P
EPS = 1e-6
MOD = 6 * NC
SH_A, SC_A, G_A, SH_F, SC_F, G_F = (NC * j for j in range(6))
UF, UQ, UK, UV, UFF, UFB, UI, UHQ, UG, UN = 0, 2, 6, 7, 8, 10, 12, 14, 16, 18
LEVELS = 7
SCALE = HD ** -0.5
NEG = -1e30


def column_map():
    at, n = {}, 0
    for name, width in (
        ("b_ada", DEPTH * MOD), ("q_norm", DEPTH), ("k_norm", DEPTH), ("hg_norm", DEPTH), ("lb", 2 * DEPTH * 2),
        ("final", NC), ("pre", DEPTH * 3 * NC), ("post", DEPTH * 3 * NC), ("conv_w", 4 * 4), ("conv_b", 4),
        ("ba", 4), ("bx", 4), ("lam", 4), ("c_conv", 3 * NC),
    ):
        at[name] = n
        n += width
    return at, n


COL, NCOL = column_map()


class Ticket:

    def __init__(self, sem, c, k=0, i=None):
        self.sem, self.c, self.k, self.i = sem, c, k, i

    def value(self):
        return self.i * self.k + self.c if self.k else self.c

    def at(self, step):
        return Ticket(self.sem, self.c + self.k * step)


class Carry:

    def __init__(self, book):
        self.t, self.stamp = [], None
        book.carries.append(self)
        self.book = book

    def set(self, *t):
        self.t, self.stamp = list(t), self.book.loop

    def add(self, *t):
        if self.stamp is not self.book.loop:
            self.t = []
        self.t, self.stamp = self.t + list(t), self.book.loop


class Book:
    def __init__(self, nc):
        self.nc, self.engines, self.carries, self.loop, self.dry = nc, [], [], None, False

    def repeat(self, steps, body, peel=False):
        if steps == 1:
            body(0)
            return
        first = 0
        if peel:
            body(0)
            first = 1
        before = [(c, list(c.t), c.stamp) for c in self.carries]
        base = {e: e.n for e in self.engines}
        known = {e: dict(e.known) for e in self.engines}
        self.loop, self.dry = {"guards": [], "final": {}, "per": {}, "i": None, "first": first}, True
        loop = self.loop
        body(0)
        per = {e.sem: e.n - base[e] for e in self.engines}
        final = {c: list(c.t) for c in self.carries if c.stamp is loop}
        for c, t, stamp in before:
            c.t, c.stamp = t, stamp
        for e in self.engines:
            e.n, e.known = base[e], known[e]
        for c, t in final.items():
            final[c] = [Ticket(x.sem, x.c - per[x.sem] * first) if x.sem in per else x for x in t]
        self.loop, self.dry = None, False
        for engine, carry in loop["guards"]:
            if carry in final:
                engine.wait(*carry.t)
        for e in self.engines:
            e.flush()
        with self.nc.Fori(first, steps) as i:
            loop.update(per=per, final=final, i=i)
            self.loop = loop
            body(i)
            for e in self.engines:
                e.flush()
        self.loop = None
        for c in self.carries:
            if c.stamp is loop:
                c.t, c.stamp = [t.at(steps - 1) for t in c.t], None
        for e in self.engines:
            assert e.n == base[e] + per[e.sem]
            e.n = base[e] + (steps - first) * per[e.sem]
            e.near = {}


class Engine:

    def __init__(self, book, engine, sem):
        self.book, self.e, self.sem, self.n, self.known, self.near = book, engine, sem, 0, {}, {}
        self.pending = []
        book.engines.append(self)

    def do(self, op, *args, inc=True, sem=None, **kw):
        if not self.book.dry:
            self.flush(op.__name__ in ("activation", "copy_predicated"))
            ins = op(*args, **kw)
            if sem is not None:
                ins.then_inc(sem, 1)
            elif inc:
                ins.then_inc(self.sem, 1)
        if sem is not None or not inc:
            return None
        self.n += 1
        loop = self.book.loop
        if loop is None:
            return Ticket(self.sem, self.n)
        per = loop["per"].get(self.sem, 0)
        return Ticket(self.sem, self.n - per * loop["first"], per, loop["i"])

    def wait(self, *tickets):
        if self.book.dry:
            return
        for t in tickets:
            if t is None:
                continue
            seen = self.near.get(t.sem) if t.k else self.known.get(t.sem)
            if t.k and (seen is None or seen[0] is not self.book.loop or seen[1] < t.c) or \
                    not t.k and (seen is None or seen < t.c):
                self.pending.append(t)
                if t.k:
                    self.near[t.sem] = (self.book.loop, t.c)
                else:
                    self.known[t.sem] = t.c

    def flush(self, fence=False):
        for t in self.pending:
            self.e.wait_ge(t.sem, t.value())
        if fence and any(t.k for t in self.pending):
            self.e.nop(nofuse=True)
        self.pending = []

    def take(self, carry):
        loop = self.book.loop
        if loop is None or carry.stamp is loop:
            self.wait(*carry.t)
        elif self.book.dry:
            loop["guards"].append((self, carry))
        elif carry in loop["final"]:
            self.wait(*[Ticket(t.sem, t.c - loop["per"][t.sem], loop["per"][t.sem], loop["i"])
                        if t.sem in loop["per"] else t for t in loop["final"][carry]])
        else:
            self.wait(*carry.t)


def ds(start, n):
    return slice(start, start + n) if isinstance(start, int) else bass.ds(start, n)


def program(nc, xT, cvec, cols, panels, ada_panels, w_four, lru_gates, mats, rope1, rope2, dft_x, dft_c, masks,
            causal, head_mask, out):
    n_panels = panels.shape[0]
    stack = ExitStack()
    with stack:
        def sb(name, shape, dt=F32, scope=stack):
            return scope.enter_context(nc.sbuf_tensor(name, shape, dt))

        def semaphore(name):
            return stack.enter_context(nc.semaphore(name))

        book = Book(nc)
        T = Engine(book, nc.tensor, semaphore("tensor_done"))
        A = Engine(book, nc.scalar, semaphore("scalar_done"))
        V = Engine(book, nc.vector, semaphore("vector_done"))
        G = Engine(book, nc.gpsimd, semaphore("gpsimd_done"))
        SP = nc.sync
        te, ac, ve, gp = nc.tensor, nc.scalar, nc.vector, nc.gpsimd
        raw_in = [semaphore(f"panel_landed_{s}") for s in range(2)]
        high_done, low_done = semaphore("panel_high"), semaphore("panel_low")
        ada_in = [semaphore(f"ada_landed_{s}") for s in range(8)]

        X = sb("X", [P, NC, TOK])
        raw = sb("raw", [P, 2, PANEL])
        WH = [sb(f"WH{s}", [P, NC, 2 * P], F32R) for s in range(2)]
        WL = [sb(f"WL{s}", [P, NC, 2 * P], F32R) for s in range(2)]
        C = sb("C", [P, NCOL])
        M = sb("M", [P, mats.shape[1], P])
        mod = sb("mod", [P, DEPTH, MOD, 2])
        SQ = [sb(f"SQ{s}", [P, TOK]) for s in range(2)]
        SS = sb("SS", [P, TOK])
        RS = sb("RS", [P, TOK])
        eps = sb("eps", [P, 1])
        one = sb("one", [P, 1])
        RC = sb("RC", [P, TOK // P])
        HM = sb("HM", [P, 2])
        PS = stack.enter_context(nc.psum_tensor("PS", [P, 8, BANK], F32))
        bank = [Carry(book) for _ in range(8)]
        c_SQ, c_RS, c_SS, c_X = [Carry(book), Carry(book)], Carry(book), Carry(book), Carry(book)
        ONES, EYE, BO, RQ, D0, D1, R0, R1, R2, DC, DS = (M[:, j, :] for j in range(11))
        stack.enter_context(nc.Block())

        loads = [0]

        def load(eng, *pairs):
            sem = semaphore(f"load_{loads[0]}")
            loads[0] += 1
            eng.flush()
            for dst, src in pairs:
                eng.e.dma_start(dst, src).then_inc(sem, 16)
            return Ticket(sem, 16 * len(pairs))

        def col(name, j=0, n=1):
            return C[:, ds(COL[name] + j, n)]

        def everyone(*engines):
            return [Ticket(e.sem, e.n) for e in (engines or (T, A, V, G))]

        for s in range(2):
            SP.dma_start(raw[:, s, :], panels[s]).then_inc(raw_in[s], 16)
        with nc.sync.Fori(1, n_panels // 2) as i:
            for s in range(2):
                SP.wait_ge(low_done, i * 2 + (s - 1))
                SP.dma_start(raw[:, s, :], panels[bass.ds(i * 2 + s, 1)].rearrange("a p n -> p (a n)"))\
                    .then_inc(raw_in[s], 16)

        t_const = load(G, (C[:], cols), (M[:], mats), (HM[:], head_mask))
        t_eps = V.do(ve.memset, eps[:], EPS)
        t_one = V.do(ve.memset, one[:], 1.0)
        t_cv_x = load(A, (X[:, :, :], xT))

        split_n = [0]
        used = [Carry(book), Carry(book)]

        def split(offset=0):
            n = split_n[0] + offset
            loop = book.loop
            k, i = (1, loop["i"]) if loop else (0, None)
            s = n % 2
            A.wait(Ticket(raw_in[s], 16 * (n // 2 + 1), 16 * k, i))
            A.take(used[s])
            A.do(ac.activation, WH[s].rearrange("p k n -> p (k n)"), raw[:, s, :], ACT.Copy, sem=high_done)
            V.wait(Ticket(high_done, n + 1, 2 * k, i))
            V.do(ve.tensor_tensor, WL[s].rearrange("p k n -> p (k n)"), raw[:, s, :],
                 WH[s].bitcast(F32).rearrange("p k n -> p (k n)"), ALU.subtract, sem=low_done)

        def panel(n_local, nk, rhs, ready, ctx, epilogue, p, last, beside=None):
            n = split_n[0] + n_local
            s = n % 2
            loop = book.loop
            k2, i = (2, loop["i"]) if loop else (0, None)
            if not last:
                split(n_local + 1)
            XH, XL = rhs
            for j in range(2):
                if beside:
                    beside(j)
                T.wait(Ticket(low_done, n + 1, k2, i))
                T.take(bank[j])
                if ctx:
                    T.take(bank[2 + j])
                for k in range(nk):
                    T.wait(*ready(k))
                    for q, (w, x) in enumerate(((WH, XH), (WH, XL), (WL, XH))):
                        st, sp = k == 0 and q == 0, k == nk - 1 and q == 2
                        lhsT = w[s][:, k, j * P:(j + 1) * P]
                        t = T.do(te.matmul, PS[:, j, :], lhsT, x[:, k, 0:SEQ], start=st, stop=sp, inc=sp and not ctx)
                        if ctx:
                            t = T.do(te.matmul, PS[:, 2 + j, 0:CTX], lhsT, x[:, k, SEQ:TOK], start=st, stop=sp,
                                     inc=sp)
                bank[j].set(t)
                if ctx:
                    bank[2 + j].set(t)
                if j == 1:
                    used[s].set(t)
                epilogue(p * 2 + j, j, t)

        def gemm(n, nk, rhs, ready, ctx, epilogue, final=False, first=0, beside=None):
            pairs = n // 2 - (1 if final else 0)
            if pairs == 1:
                for u in range(2):
                    panel(u, nk, rhs, ready, ctx, epilogue, first + u, False)
            elif pairs > 1:
                def body(i):
                    for u in range(2):
                        panel(u, nk, rhs, ready, ctx, epilogue, i * 2 + (first + u), False,
                              (lambda j: beside(i, 2 * u + j)) if beside else None)
                    if beside:
                        beside(i, 4)
                book.repeat(pairs, body, pairs > 2)
            split_n[0] += 2 * pairs
            left = n - 2 * pairs
            for u in range(left):
                panel(0, nk, rhs, ready, ctx, epilogue, first + 2 * pairs + u, final and u == left - 1)
                split_n[0] += 1

        def spans(ctx):
            return [(0, SEQ, 0), (SEQ, TOK, 1)] if ctx else [(0, SEQ, 0)]

        def squares_begin(ctx):
            V.take(c_SS)
            c_SS.set(V.do(ve.memset, SS[:, 0:TOK if ctx else SEQ], 0.0))

        def squares(src, u, ctx, *ready, chunk=None):
            N = TOK if ctx else SEQ
            A.wait(*ready)
            A.take(c_SQ[u])
            t = A.do(ac.activation, SQ[u][:, 0:N].unsqueeze(1), src, ACT.Square)
            if chunk is not None:
                c_SQ[u].set(t)
                squares_sum(u, chunk, ctx)
                return t
            V.wait(t)
            V.take(c_SS)
            t2 = V.do(ve.tensor_tensor, SS[:, 0:N], SS[:, 0:N], SQ[u][:, 0:N], ALU.add)
            c_SQ[u].set(t2)
            c_SS.set(t2)
            return t

        sums = []

        def squares_sum(u, c, ctx):
            if c == 0:
                T.take(bank[6])
                T.take(bank[7])
            T.take(c_SQ[u])
            for a, b, q in spans(ctx):
                t = T.do(te.matmul, PS[:, 6 + q, 0:b - a], ONES, SQ[u][:, a:b], start=c == 0, stop=c == NC - 1)
            c_SQ[u].set(t)
            sums.append(t)

        def squares_end(ctx):
            n = (TOK if ctx else SEQ) // P
            flat = PS[:, 6:8, :].rearrange("p b n -> p (b n)")[:, 0:n * P]
            scale = 1.0 / D
            if sums:
                A.wait(sums[-1])
                A.take(c_SS)
                t = A.do(ac.activation, SS[:, 0:n * P], flat, ACT.Copy)
                c_SS.set(t)
                scale = 1.0 / P
                bank[6].set(t)
                bank[7].set(t)
                sums.clear()
            T.take(c_SS)
            T.take(bank[5])
            T.wait(t_one)
            for j in range(n):
                t = T.do(te.matmul, PS[:, 5, j:j + 1], SS[:, j * P:(j + 1) * P], one[:], start=True, stop=True,
                         inc=j == n - 1)
            c_SS.set(t)
            A.wait(t, t_eps)
            t = A.do(ac.activation, RC[:, 0:n], PS[:, 5, 0:n], ACT.Sqrt, bias=eps[:], scale=scale)
            bank[5].set(t)
            V.wait(t)
            t = V.do(ve.reciprocal, RC[:, 0:n], RC[:, 0:n])
            T.wait(t)
            T.take(bank[6])
            T.take(bank[7])
            for j in range(n):
                t = T.do(te.matmul, PS[:, 6 + j // 4, (j % 4) * P:(j % 4 + 1) * P],
                         RC[:, j:j + 1].broadcast_to([P, P]), EYE, start=True, stop=True, inc=j == n - 1)
            A.wait(t)
            A.take(c_RS)
            t = A.do(ac.activation, RS[:, 0:n * P], flat, ACT.Copy)
            bank[6].set(t)
            bank[7].set(t)
            c_RS.set(t)

        def inverse_root(b, N, t):
            A.wait(t, t_eps)
            A.take(c_RS)
            flat = PS[:, b:b + 2, :].rearrange("p b n -> p (b n)")
            t = A.do(ac.activation, RS[:, 0:N], flat[:, 0:N], ACT.Sqrt, bias=eps[:])
            bank[b].set(t)
            bank[b + 1].set(t)
            V.wait(t)
            t = V.do(ve.reciprocal, RS[:, 0:N], RS[:, 0:N])
            c_RS.set(t)
            return t

        def normed(XH, XL, ctx, gain, shift, free):
            tickets = []
            V.wait(*free)
            A.wait(*free)
            G.wait(*free)
            V.take(c_RS)
            V.take(c_X)

            def scale(c):
                u = c % 2
                V.take(c_SQ[u])
                for a, b, q in spans(ctx):
                    t = V.do(ve.scalar_tensor_tensor, SQ[u][:, a:b], X[:, c, a:b], gain(c, q), RS[:, a:b],
                             ALU.mult, ALU.mult)
                A.wait(t)
                for a, b, q in spans(ctx):
                    t2 = A.do(ac.activation, XH[:, c, a:b], SQ[u][:, a:b], ACT.Identity,
                              bias=shift(c, q) if shift else 0.0)
                return t, t2
            t = scale(0)
            for c in range(NC):
                u = c % 2
                t_next = scale(c + 1) if c + 1 < NC else t
                if not shift and u:
                    G.wait(t[1])
                    t = G.do(gp.tensor_tensor, XL[:, c, :], SQ[u][:, 0:SEQ], XH[:, c, :].bitcast(F32), ALU.subtract)
                else:
                    V.wait(t[1])
                    for a, b, q in spans(ctx):
                        t = V.do(ve.scalar_tensor_tensor, XL[:, c, a:b], SQ[u][:, a:b], shift(c, q) if shift else 0.0,
                                 XH[:, c, a:b].bitcast(F32), ALU.add, ALU.subtract)
                c_SQ[u].set(t)
                tickets.append(t)
                t_last, t = t_next, t_next
            c_RS.add(t_last[0])
            c_X.add(t_last[0])
            return lambda k: [tickets[k]]

        def split_chunks(XH, XL, src, n, ctx, src_ready, free):
            tickets = []
            N = TOK if ctx else SEQ
            A.wait(*free)
            V.wait(*free)
            A.wait(*src_ready)
            V.wait(*src_ready)
            for c in range(n):
                t = A.do(ac.activation, XH[:, c, 0:N], src(c)[:, 0:N], ACT.Copy)
                V.wait(t)
                tickets.append(V.do(ve.tensor_tensor, XL[:, c, 0:N], src(c)[:, 0:N],
                                    XH[:, c, 0:N].bitcast(F32), ALU.subtract))
            return lambda k: [tickets[k]]

        def modulation_buffers(tag, n, scope):
            ring = sb(f"ada_{tag}", [P, n, NC, 2 * P], F32, scope)
            AD[:] = [sb(f"AD{s}_{tag}", [P, 2, 2 * P], F32, scope) for s in range(2)]
            for s in range(2):
                c_ada[s].set(*everyone())
                c_AD[s].set(*everyone())
            return ring

        def modulation_fetch(ring, slot, n):
            G.take(c_ada[slot])
            if not book.dry:
                G.flush()
                gp.dma_start(ring[:, slot].rearrange("p k n -> p (k n)"),
                             ada_panels[ds(n, 1)].rearrange("a p n -> p (a n)")).then_inc(ada_in[slot], 16)

        def modulation_terms(ring, slot, landed, both=True):
            s = slot % 2
            V.wait(landed, t_cv)
            V.take(c_AD[s])
            t = None
            for k in range(NC):
                V.wait(t)
                for q in range(2 if both else 1):
                    if k == 0:
                        t = V.do(ve.tensor_scalar, AD[s][:, q, :], ring[:, slot, 0, :], cv[:, 0, q:q + 1], None,
                                 ALU.mult)
                    else:
                        t = V.do(ve.scalar_tensor_tensor, AD[s][:, q, :], ring[:, slot, k, :], cv[:, k, q:q + 1],
                                 AD[s][:, q, :], ALU.mult, ALU.add)
            c_ada[slot].set(t)
            c_AD[s].set(t)
            return t

        def modulation_direct(ring, slot, l, p, landed):
            T.wait(landed, t_cv)
            T.take(bank[3])
            for j in range(2):
                for k in range(NC):
                    t = T.do(te.matmul, PS[:, 3, j * 2:j * 2 + 2], ring[:, slot, k, j * P:(j + 1) * P],
                             cv[:, k, :], start=k == 0, stop=k == NC - 1, inc=k == NC - 1 and j == 1)
            c_ada[slot].set(t)
            add_bias(l, p, 3, 2, t)

        def add_bias(l, p, b, n, t):
            V.wait(t, t_const)
            bias = C[:, ds(p * 2 + (COL["b_ada"] + l * MOD), 2)].unsqueeze(2).broadcast_to([P, 2, n])
            t = V.do(ve.tensor_tensor, mod[:, l, ds(p * 2, 2), 0:n],
                     PS[:, b, 0:4].rearrange("p (a b) -> p a b", a=2)[:, :, 0:n], bias, ALU.add)
            bank[b].set(t)

        def modulation_sum(slot, l, p, terms, both=True):
            s = slot % 2
            b = 4 + s
            T.wait(terms, t_one)
            T.take(bank[b])
            for j in range(2):
                for q in range(2 if both else 1):
                    t = T.do(te.matmul, PS[:, b, 2 * j + q:2 * j + q + 1], AD[s][:, q, j * P:(j + 1) * P], one[:],
                             start=True, stop=True, inc=j == 1 and q == both)
            c_AD[s].set(t)
            add_bias(l, p, b, 2 if both else 1, t)

        def one_plus(l, sc, n=2):
            t = V.do(ve.tensor_scalar, mod[:, l, sc:sc + NC, 0:n], mod[:, l, sc:sc + NC, 0:n], 1.0, None, ALU.add)
            A.wait(t)
            V.wait(t)

        def modulation_beside(ring, l, first, rounds, pairs, both=True):
            n0 = ada_count[0]
            ada_count[0] += rounds * pairs
            plan = {1: ("F0 F1", "V0", "V1 S0", "", "S1"), 2: ("F0 F1", "V0 F2", "V1 S0 F3", "S1 V2 V3", "S2 S3")}
            terms = {}

            def beside(i, x):
                loop = book.loop
                for what in plan[rounds][x].split():
                    m = int(what[1])
                    p = i * (2 * rounds) + (first + m)
                    if what[0] == "F":
                        modulation_fetch(ring, m % 2, p + l * (MOD // 2))
                    elif what[0] == "V":
                        k, it = (16 * rounds, loop["i"]) if loop else (0, None)
                        landed = 16 * (n0 + m // 2 + 1 + (0 if loop else i * rounds))
                        terms[m] = modulation_terms(ring, m % 2, Ticket(ada_in[m % 2], landed, k, it), both)
                    else:
                        modulation_sum(m % 2, l, p, terms[m], both)
            return beside

        c_ada = [Carry(book) for _ in range(8)]
        c_AD = [Carry(book) for _ in range(2)]
        AD = []
        ada_count = [0]

        def ffn(tag, ctx, gain, shift, down, begin, final=False, ada=None):
            N = TOK if ctx else SEQ
            with ExitStack() as scope:
                XH = sb(f"XH_{tag}", [P, NC, N], F32R, scope)
                XL = sb(f"XL_{tag}", [P, NC, N], F32R, scope)
                HH = sb(f"HH_{tag}", [P, NC, N], F32R, scope)
                HL = sb(f"HL_{tag}", [P, NC, N], F32R, scope)
                GA = [sb(f"GA{s}_{tag}", [P, N], F32, scope) for s in range(1)]
                squares_end(ctx)
                begin()
                ready = normed(XH, XL, ctx, gain, shift, everyone())
                c_GA, c_hid = Carry(book), Carry(book)
                for g, nk in enumerate(GROUPS):
                    hid = Carry(book)

                    def gate_up(c, j, t, hid=hid):
                        if j == 0:
                            A.wait(t)
                            A.take(c_GA)
                            for a, b, q in spans(ctx):
                                ta = A.do(ac.activation, GA[0][:, a:b], PS[:, 2 * q, 0:b - a], ACT.Silu)
                                bank[2 * q].set(ta)
                            c_GA.set(ta)
                            return
                        m = c_of(c)
                        V.wait(t)
                        V.take(c_GA)
                        for a, b, q in spans(ctx):
                            tv = V.do(ve.tensor_tensor, GA[0][:, a:b], PS[:, 2 * q + 1, 0:b - a], GA[0][:, a:b],
                                      ALU.mult)
                            bank[2 * q + 1].set(tv)
                        A.wait(tv)
                        ta = A.do(ac.activation, HH[:, ds(m, 1), :], GA[0][:, :].unsqueeze(1), ACT.Copy)
                        V.wait(ta)
                        tv = V.do(ve.tensor_tensor, HL[:, ds(m, 1), :], GA[0][:, :].unsqueeze(1),
                                  HH[:, ds(m, 1), :].bitcast(F32), ALU.subtract)
                        c_GA.set(tv)
                        hid.set(tv)

                    def c_of(c):
                        return half[0]

                    half = [0]
                    panel_epilogue(nk, (XH, XL), ready, ctx, gate_up, half, ada(scope, g) if ada else None)
                    t_hid = hid.t

                    def ready_h(k, nk=nk, t_hid=t_hid):
                        return t_hid if k == nk - 1 else [Ticket(V.sem, t_hid[0].c - per_chunk(ctx))]

                    gemm(NC // 2, nk, (HH, HL), ready_h, ctx, lambda c, j, t, g=g: down(c, g, j, t),
                         final=final and g == len(GROUPS) - 1)
                return everyone()

        def per_chunk(ctx):
            return 3 if ctx else 2

        def panel_epilogue(nk, rhs, ready, ctx, gate_up, half, beside):
            pairs = nk // 2

            def body(i):
                for u in range(2):
                    half[0] = i * 2 + u
                    panel(u, NC, rhs, ready, ctx, gate_up, 0, False,
                          (lambda j: beside(i, 2 * u + j)) if beside else None)
                if beside:
                    beside(i, 4)
            book.repeat(pairs, body, True)
            split_n[0] += nk

        def add_to_x(l, g_col, ctx, sum_group, sum_ctx):
            def down(c, g, j, t):
                V.wait(t)
                V.take(c_X)
                for a, b, q in spans(ctx):
                    t = V.do(ve.scalar_tensor_tensor, X[:, ds(c, 1), a:b], PS[:, ds(2 * q + j, 1), 0:b - a],
                             mod[:, l, ds(c + g_col, 1), q:q + 1].rearrange("p a b -> p (a b)"),
                             X[:, ds(c, 1), a:b], ALU.mult, ALU.add)
                    bank[2 * q + j].set(t)
                if g == sum_group:
                    t = squares(X[:, ds(c, 1), 0:TOK if sum_ctx else SEQ], j, sum_ctx, t)
                c_X.set(t)
            return down

        def head_norm(dst, src, N, gain, src_t):
            A.wait(*src_t)
            A.take(c_SQ[0])
            t = A.do(ac.activation, SQ[0][:, 0:N], src, ACT.Square)
            T.wait(t)
            T.take(bank[6])
            T.take(bank[7])
            for a in range(0, N, BANK):
                b = min(N, a + BANK)
                t = T.do(te.matmul, PS[:, 6 + a // BANK, 0:b - a], BO, SQ[0][:, a:b], start=True, stop=True)
            c_SQ[0].set(t)
            inverse_root(6, N, t)
            V.take(c_RS)
            t = V.do(ve.scalar_tensor_tensor, dst, src, gain, RS[:, 0:N], ALU.mult, ALU.mult)
            c_RS.add(t)
            return t

        def rope(dst, src, N, tab, direct, rotate, t_src, t_dst):
            cos, sin = tab
            T.wait(*t_src)
            T.take(bank[6])
            T.take(bank[7])
            for a in range(0, N, BANK):
                b = min(N, a + BANK)
                t = T.do(te.matmul, PS[:, 6 + a // BANK, 0:b - a], rotate, src[:, a:b], start=True, stop=True)
            rot = PS[:, 6:8, :].rearrange("p b n -> p (b n)")
            V.wait(t, *t_dst)
            t = V.do(ve.tensor_tensor, dst, rot[:, 0:N], sin[:, 0:N], ALU.mult)
            if direct is not None:
                T.wait(t)
                for a in range(0, N, BANK):
                    b = min(N, a + BANK)
                    td = T.do(te.matmul, PS[:, 6 + a // BANK, 0:b - a], direct, src[:, a:b], start=True, stop=True)
                V.wait(td)
            plain = src if direct is None else rot[:, 0:N]
            V.take(c_SQ[1])
            V.wait(*t_src)
            t2 = V.do(ve.tensor_tensor, SQ[1][:, 0:N], plain, cos[:, 0:N], ALU.mult)
            bank[6].set(t2)
            bank[7].set(t2)
            V.wait(t2)
            t = V.do(ve.tensor_tensor, dst, dst, SQ[1][:, 0:N], ALU.add)
            c_SQ[1].set(t)
            return t

        def head_halves(dst, src, t_src, t_dst):
            V.wait(t_src, *t_dst)
            for h in range(2):
                t = V.do(ve.tensor_scalar, dst[h], src, HM[:, h:h + 1], None, ALU.mult)
            return t

        def attend(scope, tag, dest, n_chunks, prep, tiles, K, Vt, v_half, groups, t_kv, t_mask,
                   mask):
            QR = sb(f"QR_{tag}", [P, TOK], F32, scope)
            PB = [sb(f"PB{s}_{tag}", [P, TOK], F32, scope) for s in range(2)]
            PT = [sb(f"PT{s}_{tag}", [P, TOK], F32, scope) for s in range(2)]
            OT = [sb(f"OT{s}_{tag}", [P, P], F32, scope) for s in range(2)]
            nmax = [sb(f"nmax{s}_{tag}", [P, 1], F32, scope) for s in range(2)]
            rsum = [sb(f"rsum{s}_{tag}", [P, 1], F32, scope) for s in range(2)]
            rinv = [sb(f"rinv{s}_{tag}", [P, 1], F32, scope) for s in range(2)]
            c_QR = Carry(book)
            c_PB, c_PT, c_OT = ([Carry(book), Carry(book)] for _ in range(3))
            c_nm, c_rs = ([Carry(book), Carry(book)] for _ in range(2))
            steps = [(q0, k0, nk, dm, h) for q0, k0, nk, dm in tiles for h in range(2)]

            for grp in range(groups):
                kv_of = (lambda c: grp) if groups > 1 else (lambda c: c)

                def body(i, grp=grp):
                    c = i + grp * (n_chunks // groups)
                    V.take(c_QR)
                    A.take(c_QR)
                    t_q = prep(QR, c)
                    c_QR.set(t_q)

                    def scores(x):
                        q0, k0, nk, dm, h = steps[x]
                        b = x % 2
                        T.wait(t_q, *t_kv)
                        T.take(bank[2 * b])
                        T.take(bank[2 * b + 1])
                        for a in range(0, nk, BANK):
                            n = min(BANK, nk - a)
                            t = T.do(te.matmul, PS[:, 2 * b + a // BANK, 0:n], QR[:, q0:q0 + P],
                                     K(grp, h, k0 + a, n), start=True, stop=True)
                        c_QR.add(t)
                        S = PS[:, 2 * b:2 * b + 2, :].rearrange("p b n -> p (b n)")[:, 0:nk]
                        V.wait(t)
                        if dm:
                            V.wait(t_mask)
                            t = V.do(ve.tensor_tensor, S[:, nk - P:nk], S[:, nk - P:nk], mask, ALU.add)
                            V.wait(t)
                        V.take(c_nm[b])
                        t = V.do(ve.tensor_reduce, nmax[b][:], S, AX_X, ALU.max)
                        V.wait(t)
                        t = V.do(ve.tensor_scalar, nmax[b][:], nmax[b][:], -SCALE, None, ALU.mult)
                        A.wait(t)
                        A.take(c_PB[b])
                        A.take(c_rs[b])
                        t = A.do(ac.activation, PB[b][:, 0:nk], S, ACT.Exp, bias=nmax[b][:], scale=SCALE,
                                 accum_out=rsum[b][:])
                        c_nm[b].set(t)
                        bank[2 * b].set(t)
                        bank[2 * b + 1].set(t)
                        return t

                    def turn(x, t_exp):
                        q0, k0, nk, dm, h = steps[x]
                        b, nkt = x % 2, nk // P
                        low = nkt // 2
                        T.wait(t_exp)
                        T.take(bank[4])
                        T.take(bank[5])
                        for kt in range(nkt):
                            to = PS[:, 4, kt * P:(kt + 1) * P] if kt < low else \
                                PS[:, 5, (kt - low) * P:(kt - low + 1) * P]
                            t = T.do(te.transpose, to, PB[b][:, kt * P:(kt + 1) * P], EYE,
                                     inc=kt in (low - 1, nkt - 1))
                            if kt == low - 1:
                                t_half = t
                        c_PB[b].set(t)
                        half, done = low * P, []
                        if half:
                            A.wait(t_half)
                            A.take(c_PT[b])
                            done.append(A.do(ac.activation, PT[b][:, 0:half], PS[:, 4, 0:half], ACT.Copy))
                            bank[4].set(*done)
                        V.wait(t)
                        V.take(c_PT[b])
                        done.append(V.do(ve.tensor_copy, PT[b][:, half:nk], PS[:, 5, 0:nk - half]))
                        bank[5].set(done[-1])
                        V.wait(t_exp)
                        V.take(c_rs[b])
                        return done, V.do(ve.reciprocal, rinv[b][:], rsum[b][:])

                    def values(x, turned):
                        q0, k0, nk, dm, h = steps[x]
                        b, nkt = x % 2, nk // P
                        done, t_inv = turned
                        T.wait(*done)
                        T.take(bank[6])
                        for kt in range(nkt):
                            t = T.do(te.matmul, PS[:, 6, 0:P], PT[b][:, kt * P:(kt + 1) * P],
                                     Vt(kv_of(c), k0 // P + kt), start=kt == 0, stop=kt == nkt - 1,
                                     inc=kt == nkt - 1)
                        c_PT[b].set(t)
                        ob = (x // 2) % 2
                        V.wait(t, t_inv)
                        if h == 0:
                            V.take(c_OT[ob])
                        v0 = v_half(grp, h) * HD
                        t = V.do(ve.tensor_scalar, OT[ob][:, h * HD:(h + 1) * HD], PS[:, 6, v0:v0 + HD], rinv[b][:],
                                 None, ALU.mult)
                        c_rs[b].set(t)
                        bank[6].set(t)
                        return (ob, q0, t) if h == 1 else None

                    def turn_back(ob, q0, t):
                        T.wait(t)
                        T.take(bank[7])
                        t = T.do(te.transpose, PS[:, 7, 0:P], OT[ob][:, :], EYE)
                        c_OT[ob].set(t)
                        A.wait(t)
                        t = A.do(ac.activation, dest(c, q0), PS[:, 7, 0:P].unsqueeze(1), ACT.Copy)
                        bank[7].set(t)

                    n = len(steps)
                    exps, turns, back = {}, {}, None
                    for x in range(-2, n):
                        if x + 2 < n:
                            exps[x + 2] = scores(x + 2)
                        if 0 <= x + 1 < n:
                            turns[x + 1] = turn(x + 1, exps[x + 1])
                        if back:
                            turn_back(*back)
                        back = values(x, turns[x]) if x >= 0 else None
                    turn_back(*back)
                book.repeat(n_chunks // groups, body)

        def token_major(dst, src, n, t_src, t_dst):
            T.wait(*t_src)
            A.wait(*t_dst)
            for j in range(n):
                b = 4 + j % 2
                T.take(bank[b])
                t = T.do(te.transpose, PS[:, b, 0:P], src(j), EYE)
                A.wait(t)
                t = A.do(ac.activation, dst(j), PS[:, b, 0:P], ACT.Copy)
                bank[b].set(t)
            return t

        def fourier(l, U, ctx, t_in):
            with ExitStack() as scope:
                AB = sb(f"AB_{l}", [P, TOK // P, 2, 2, P], F32, scope)
                WF = sb(f"WF_{l}", [P, 2, 2 * P], F32, scope)
                Z = sb(f"Z_{l}", [P, 2, SEQ], F32, scope)
                FX = sb(f"FX_{l}", [P, 2, SEQ // P, SEQ], F32, scope)
                FC = sb(f"FC_{l}", [P, 2, CTX // P, CTX], F32, scope)
                G.wait(*t_in)
                t_tab = load(G, (WF[:], w_four[l]), (FX[:], dft_x), (FC[:], dft_c))
                T.wait(*t_in)
                A.wait(*t_in)
                V.wait(*t_in)
                t_ab = None
                for tt in range((TOK if ctx else SEQ) // P):
                    b = 4 + tt % 2
                    T.take(bank[b])
                    for fc in range(2):
                        for cs, W in enumerate((DC, DS)):
                            t = T.do(te.matmul, PS[:, b, (2 * fc + cs) * P:(2 * fc + cs + 1) * P],
                                     U[:, UF + fc, tt * P:(tt + 1) * P], W, start=True, stop=True)
                    A.wait(t)
                    t_ab = A.do(ac.activation, AB[:, tt].rearrange("p a b n -> p (a b n)"), PS[:, b, :], ACT.Copy)
                    bank[b].set(t_ab)
                for a, n, tab in ((0, SEQ, FX), (SEQ, CTX, FC))[:2 if ctx else 1]:
                    nt = n // P
                    T.wait(t_ab, t_tab)
                    for fc in range(2):
                        T.take(bank[fc])
                        for x in range(2 * nt):
                            t = T.do(te.matmul, PS[:, fc, 0:n], AB[:, a // P + x // 2, fc, x % 2, :],
                                     tab[:, x % 2, x // 2, :], start=x == 0, stop=x == 2 * nt - 1)
                        V.wait(t)
                        tz = V.do(ve.tensor_copy, Z[:, fc, 0:n], PS[:, fc, 0:n])
                        bank[fc].set(tz)
                    T.wait(tz)
                    for m in range(2):
                        T.take(bank[2 + m])
                        for fc in range(2):
                            t = T.do(te.matmul, PS[:, 2 + m, 0:n], WF[:, fc, m * P:(m + 1) * P], Z[:, fc, 0:n],
                                     start=fc == 0, stop=fc == 1)
                        V.wait(t)
                        tz = V.do(ve.tensor_copy, U[:, UF + m, a:a + n], PS[:, 2 + m, 0:n])
                        bank[2 + m].set(tz)
                    V.wait(t)
            return everyone()

        def attention1(l, U, ctx, t_in):
            with ExitStack() as scope:
                tab = sb(f"rope_{l}", [P, 2, TOK], F32, scope)
                KK = [[sb(f"KK{kv}{h}_{l}", [P, TOK], F32, scope) for h in range(2)] for kv in range(2)]
                kr = sb(f"kr_{l}", [P, TOK], F32, scope)
                VT = sb(f"VT_{l}", [P, TOK // P, P], F32, scope)
                qn = sb(f"qn_{l}", [P, TOK], F32, scope)
                for e in (T, A, V, G):
                    e.wait(*t_in)
                t_tab = load(G, (tab[:], rope1))
                T.wait(t_tab)
                V.wait(t_tab)
                cs = (tab[:, 0, :], tab[:, 1, :])
                t_k = head_norm(qn[:], U[:, UK, :], TOK, col("k_norm", l), [])
                t_kk = None
                for kv, (direct, rotate) in enumerate(((D0, R0), (D1, R1))):
                    t_kr = rope(kr[:], qn[:, :], TOK, cs, direct, rotate, [t_k], [t_kk])
                    t_kk = head_halves([k[:] for k in KK[kv]], kr[:], t_kr, [])
                t_v = token_major(lambda j: VT[:, j, :], lambda j: U[:, UV, j * P:(j + 1) * P], TOK // P, [], [])
                c_qn = Carry(book)
                c_qn.set(t_kk)
                N = TOK if ctx else SEQ

                def prep(QR, c):
                    V.take(c_qn)
                    src = U[:, ds(c + UQ, 1), 0:N].rearrange("p a n -> p (a n)")
                    t = head_norm(qn[:, 0:N], src, N, col("q_norm", l), [])
                    t = rope(QR[:, 0:N], qn[:, 0:N], N, cs, None, RQ, [t], [])
                    c_qn.set(t)
                    return t

                tiles = [(q, 0, TOK, False) for q in range(0, SEQ, P)]
                if ctx:
                    tiles += [(q, SEQ, CTX, False) for q in range(SEQ, TOK, P)]
                attend(scope, f"a{l}", lambda c, q0: U[:, ds(c + UQ, 1), q0:q0 + P], 4, prep, tiles,
                       lambda kv, h, k0, n: KK[kv][h][:, k0:k0 + n], lambda kv, kt: VT[:, kt, :],
                       lambda kv, h: kv, 2, [t_kk, t_v], None, None)
            return everyone()

        def hgrn(l, U, ctx, t_in):
            NT = TOK // P
            with ExitStack() as scope:
                cum = sb(f"cum_{l}", [P, 2, 2, TOK], F32, scope)
                E = [sb(f"E{d}_{l}", [P, LEVELS + 2, 2, P], F32, scope) for d in range(2)]
                VT = sb(f"hVT_{l}", [P, NT, 2 * P], F32, scope)
                VS = [sb(f"VS{d}_{l}", [P, 2, 4, HD], F32, scope) for d in range(2)]
                WZ = [sb(f"WZ{d}_{l}", [P, 4, 2, 2, P], F32, scope) for d in range(2)]
                KT = [sb(f"KT{d}_{l}", [P, 2 * P], F32, scope) for d in range(2)]
                att = [sb(f"att{d}_{l}", [P, 4, P], F32, scope) for d in range(2)]
                MK = sb(f"MK_{l}", [P, 2, LEVELS, P], U8, scope)
                S = [sb(f"S{d}_{l}", [P, 2, P], F32, scope) for d in range(2)]
                el = [sb(f"el{d}_{l}", [P, 2], F32, scope) for d in range(2)]
                lb = sb(f"lb_{l}", [P, 2, 2], F32, scope)
                oml = sb(f"oml_{l}", [P, 2, 2], F32, scope)
                O = sb(f"O_{l}", [P, 2, TOK], F32, scope)
                for e in (T, A, V, G):
                    e.wait(*t_in)
                t_mk = load(G, (WZ[0][:].rearrange("p a b h n -> p (a b h n)")[:, 0:2 * LEVELS * P],
                                masks.rearrange("p d l n -> p (d l n)")))
                t_v = token_major(lambda j: VT[:, j // 2, (j % 2) * P:(j % 2 + 1) * P],
                                  lambda j: U[:, UI + j % 2, (j // 2) * P:(j // 2 + 1) * P], 2 * NT, [], [])
                if l == 0:
                    t_lb = V.do(ve.memset, lb[:], 0.0)
                else:
                    d01 = C[:, ds(COL["lb"], 8)].rearrange("p (d l f) -> p d l f", d=2, l=2)
                    t = V.do(ve.tensor_tensor, lb[:], d01[:, :, 1, :], d01[:, :, 0, :], ALU.subtract)
                    A.wait(t)
                    t_lb = A.do(ac.activation, lb[:], lb[:], ACT.Sigmoid)
                V.wait(t_lb)
                t_lb = V.do(ve.tensor_scalar, oml[:], lb[:], -1.0, 1.0, ALU.mult, ALU.add)
                t_f = []
                for d in range(2):
                    for fc in range(2):
                        z = U[:, UFF + 2 * d + fc, :]
                        Et = E[d][:].rearrange("p a b n -> p (a b n)")[:, fc * TOK:(fc + 1) * TOK]
                        t = A.do(ac.activation, Et, z, ACT.Sigmoid)
                        A.wait(t)
                        t2 = A.do(ac.activation, z, z, ACT.Sigmoid, scale=-1.0)
                        V.wait(t, t_lb)
                        t = V.do(ve.tensor_scalar, Et, Et, oml[:, d, fc:fc + 1], lb[:, d, fc:fc + 1],
                                 ALU.mult, ALU.add)
                        V.wait(t)
                        t = V.do(ve.tensor_scalar, Et, Et, 2.0 ** -63, None, ALU.max)
                        t_f.append(t)
                        V.wait(t2)
                        t_k = V.do(ve.tensor_scalar, z, z, oml[:, d, fc:fc + 1], None, ALU.mult)
                tm = V.do(ve.memset, SQ[0][:], 1.0)
                V.wait(tm)
                tm = V.do(ve.memset, SQ[0][:].rearrange("p (j t) -> p j t", t=P)[:, :, 0:1], 0.0)
                V.wait(tm)
                tm = V.do(ve.memset, SQ[1][:], 1.0)
                V.wait(tm)
                tm = V.do(ve.memset, SQ[1][:].rearrange("p (j t) -> p j t", t=P)[:, :, P - 1:P], 0.0)
                V.wait(tm)
                for d in range(2):
                    for fc in range(2):
                        Et = E[d][:].rearrange("p a b n -> p (a b n)")[:, fc * TOK:(fc + 1) * TOK]
                        A.wait(t_f[2 * d + fc])
                        t = A.do(ac.activation, Et, Et, ACT.Ln)
                        V.wait(t)
                        st = 1 if d == 0 else -1
                        t_cum = V.do(ve.tensor_tensor_scan, cum[:, d, fc, ::st], SQ[d][:, ::st], Et[:, ::st], 0.0,
                                     ALU.mult, ALU.add)
                c_SQ[0].set(t_cum)
                c_SQ[1].set(t_cum)
                V.wait(t_mk)
                t_mk = V.do(ve.tensor_copy, MK[:].rearrange("p d l n -> p (d l n)"),
                            WZ[0][:].rearrange("p a b h n -> p (a b h n)")[:, 0:2 * LEVELS * P])
                N = TOK if ctx else SEQ
                V.wait(t_k)
                for fc in range(2):
                    t = V.do(ve.tensor_tensor, O[:, fc, 0:N], U[:, UFF + fc, 0:N], U[:, UFB + fc, 0:N], ALU.add)
                    V.wait(t)
                    t = V.do(ve.tensor_tensor, O[:, fc, 0:N], O[:, fc, 0:N], U[:, UHQ + fc, 0:N], ALU.mult)
                    T.wait(t)
                    T.take(bank[6])
                    T.take(bank[7])
                    for a in range(0, N, BANK):
                        b = min(N, a + BANK)
                        t = T.do(te.matmul, PS[:, 6 + a // BANK, 0:b - a], BO, O[:, fc, a:b], start=True, stop=True)
                    V.wait(t)
                    t_o = V.do(ve.scalar_tensor_tensor, O[:, fc, 0:N],
                               PS[:, 6:8, :].rearrange("p b n -> p (b n)")[:, 0:N], float(HD), U[:, UI + fc, 0:N],
                               ALU.mult, ALU.mult)
                    bank[6].set(t_o)
                    bank[7].set(t_o)
                c_O, c_S = Carry(book), [Carry(book), Carry(book)]
                c_O.set(t_o)
                c_E, c_att, c_VS, c_KT, c_el = ([Carry(book), Carry(book)] for _ in range(5))
                for d in range(2):
                    t = V.do(ve.memset, att[d][:], 0.0)
                    c_att[d].set(t)
                    V.do(ve.memset, VS[d][:], 0.0)
                    t = V.do(ve.memset, S[d][:], 0.0)
                    c_S[d].set(t)
                    c_E[d].set(t_cum)
                for e in (T, A, V, G):
                    e.wait(t_mk, t_cum, t_k, t_v, t_o, t)

                def halves(ap, h):
                    return ap.rearrange("p f (b t) -> p f b t", t=2 * h)

                c_WZ = [Carry(book), Carry(book)]

                def pair(js, with_out):
                    W = [dict(), dict()]
                    for d in range(2):
                        exponents(d, js[d], with_out, W[d])
                    for d in range(2):
                        factors(d, js[d], with_out, W[d])
                    if with_out:
                        for g0, g1 in ((0, 4), (4, LEVELS)):
                            for d in range(2):
                                head_parts(d, g0, g1, W[d])
                            for lv in range(g0, g1):
                                for d in range(2):
                                    level(d, lv, g0, W[d])
                    for d in range(2):
                        turn_keys(d, W[d])
                    for d in range(2):
                        if with_out:
                            outputs(d, js[d], W[d])
                        next_state(d, W[d])

                def sides(d, h):
                    return (slice(h, 2 * h), slice(0, h)) if d == 0 else (slice(0, h), slice(h, 2 * h))

                def exponents(d, j, with_out, w):
                    cu, Ed = cum[:, d, :, ds(j * P, P)], E[d]
                    V.take(c_E[d])
                    A.take(c_E[d])
                    edge = P - 1 if d == 0 else 0
                    if with_out:
                        for lv in range(LEVELS):
                            h = P >> (lv + 1)
                            src, dst = halves(cu, h), halves(Ed[:, lv], h)
                            mid = h - 1 if d == 0 else h
                            ref = src[:, :, :, mid:mid + 1].broadcast_to([P, 2, P // (2 * h), h])
                            late, early = sides(d, h)
                            V.do(ve.tensor_tensor, dst[:, :, :, late], src[:, :, :, late], ref, ALU.subtract)
                            w["lv"] = V.do(ve.tensor_tensor, dst[:, :, :, early], ref, src[:, :, :, early],
                                           ALU.subtract)
                    w["end"] = V.do(ve.tensor_tensor, Ed[:, LEVELS + 1],
                                    cu[:, :, edge:edge + 1].broadcast_to([P, 2, P]), cu, ALU.subtract)
                    A.take(c_el[d])
                    w["el"] = A.do(ac.activation, el[d][:], cu[:, :, edge], ACT.Exp)
                    if with_out:
                        w["start"] = A.do(ac.activation, Ed[:, LEVELS], cu, ACT.Exp)
                        A.wait(w["lv"])
                        w["exp"] = A.do(ac.activation, Ed[:, 0:LEVELS], Ed[:, 0:LEVELS], ACT.Exp)
                    A.wait(w["end"])
                    w["end"] = A.do(ac.activation, Ed[:, LEVELS + 1], Ed[:, LEVELS + 1], ACT.Exp)

                def factors(d, j, with_out, w):
                    tok, Ed = ds(j * P, P), E[d]
                    q, k = U[:, UHQ:UHQ + 2, tok], U[:, UFF + 2 * d:UFF + 2 * d + 2, tok]
                    A.take(c_VS[d])
                    for fc in range(2):
                        v = VT[:, ds(j, 1), fc * P:(fc + 1) * P].rearrange("p j (h e) -> p (j h) e", h=2)
                        w["v"] = A.do(ac.activation, VS[d][:, fc, 0:4:3, :], v, ACT.Copy)
                    if with_out:
                        G.wait(w["exp"])
                        V.wait(w["exp"])
                        w["f"] = []
                        for lv in range(LEVELS):
                            h = P >> (lv + 1)
                            ww, qq, kk = halves(Ed[:, lv], h), halves(q, h), halves(k, h)
                            late, early = sides(d, h)
                            eng, op = (V, ve.tensor_tensor) if lv in (0, 4) else (G, gp.tensor_tensor)
                            eng.do(op, ww[:, :, :, late], ww[:, :, :, late], qq[:, :, :, late], ALU.mult)
                            w["f"].append(eng.do(op, ww[:, :, :, early], ww[:, :, :, early], kk[:, :, :, early],
                                                 ALU.mult))
                        V.wait(w["start"])
                        w["qs"] = V.do(ve.tensor_tensor, Ed[:, LEVELS], Ed[:, LEVELS], q, ALU.mult)
                    V.wait(w["end"])
                    w["ke"] = V.do(ve.tensor_tensor, Ed[:, LEVELS + 1], Ed[:, LEVELS + 1], k, ALU.mult)

                def head_parts(d, g0, g1, w):
                    A.wait(*w["f"][g0:g1])
                    A.take(c_WZ[d])
                    for h in range(2):
                        w["z"] = A.do(ac.activation, WZ[d][:, 0:g1 - g0, :, h, :], E[d][:, g0:g1], ACT.Copy,
                                      scale=HM[:, h:h + 1])

                def level(d, lv, g0, w):
                    b = 2 * d + lv % 2
                    T.wait(w["z"])
                    T.take(bank[b])
                    for fc in range(2):
                        t = T.do(te.matmul, PS[:, b, fc * 2 * P:(fc + 1) * 2 * P], E[d][:, lv, fc, :],
                                 WZ[d][:, lv - g0, fc].rearrange("p h n -> p (h n)"), start=True, stop=True,
                                 inc=fc == 1)
                    c_WZ[d].set(t)
                    V.wait(t)
                    V.wait(w.get("att"))
                    if lv == 0:
                        V.take(c_att[d])
                    w["att"] = V.do(ve.copy_predicated, att[d][:],
                                    MK[:, d, lv, :].unsqueeze(1).broadcast_to([P, 4, P]),
                                    PS[:, b, :].rearrange("p (a n) -> p a n", n=P))
                    bank[b].set(w["att"])

                def turn_keys(d, w):
                    T.wait(w["ke"])
                    T.take(bank[4 + d])
                    for fc in range(2):
                        t = T.do(te.transpose, PS[:, 4 + d, fc * P:(fc + 1) * P], E[d][:, LEVELS + 1, fc, :], EYE)
                    A.wait(t)
                    A.take(c_KT[d])
                    w["kt"] = A.do(ac.activation, KT[d][:], PS[:, 4 + d, 0:2 * P], ACT.Copy)

                def outputs(d, j, w):
                    T.wait(w["att"], w["v"], w["qs"])
                    T.take(c_S[d])
                    T.take(bank[6 + d])
                    for fc in range(2):
                        to = PS[:, 6 + d, fc * P:(fc + 1) * P]
                        T.do(te.matmul, to, S[d][:, fc, :], E[d][:, LEVELS, fc, :], start=True, stop=False, inc=False)
                        for h in range(2):
                            t = T.do(te.matmul, to, VS[d][:, fc, 2 * h:2 * h + 2, :].rearrange("p a e -> p (a e)"),
                                     att[d][:, 2 * fc + h, :], start=False, stop=h == 1, inc=h == 1)
                    c_att[d].set(t)
                    c_S[d].add(t)
                    V.wait(t)
                    V.take(c_O)
                    ot = O[:, :, ds(j * P, P)]
                    t = V.do(ve.tensor_tensor, ot, PS[:, 6 + d, 0:2 * P].rearrange("p (f n) -> p f n", f=2), ot,
                             ALU.add)
                    bank[6 + d].set(t)
                    c_O.set(t)

                def next_state(d, w):
                    T.wait(w["kt"], w["v"])
                    for fc in range(2):
                        t = T.do(te.matmul, PS[:, 4 + d, 2 * P + fc * P:2 * P + (fc + 1) * P],
                                 KT[d][:, fc * P:(fc + 1) * P], VS[d][:, fc, 0:4:3, :], start=True, stop=True)
                    c_E[d].set(t)
                    c_KT[d].set(t)
                    c_VS[d].set(t)
                    V.wait(t, w["el"])
                    V.take(c_S[d])
                    for fc in range(2):
                        for hf in range(2):
                            hp = slice(hf * HD, (hf + 1) * HD)
                            t = V.do(ve.scalar_tensor_tensor, S[d][hp, fc, hf * HD:(hf + 1) * HD],
                                     S[d][hp, fc, hf * HD:(hf + 1) * HD], el[d][hp, fc:fc + 1],
                                     PS[hp, 4 + d, 2 * P + fc * P + hf * HD:2 * P + fc * P + (hf + 1) * HD],
                                     ALU.mult, ALU.add)
                    c_S[d].set(t)
                    c_el[d].set(t)
                    bank[4 + d].set(t)

                nx, nctx = SEQ // P, CTX // P


                def ctx_body(i):
                    pair((i + nx, i * -1 + (NT - 1)), ctx)

                def x_body(i):
                    pair((i, i * -1 + (nx - 1)), True)
                book.repeat(nctx, ctx_body)
                book.repeat(nx, x_body)
                A.wait(*c_O.t)
                for fc in range(2):
                    t_g = A.do(ac.activation, U[:, UG + fc, 0:N], U[:, UG + fc, 0:N], ACT.Silu)
                    t = head_norm(O[:, fc, 0:N], O[:, fc, 0:N], N, col("hg_norm", l), c_O.t)
                    V.wait(t, t_g)
                    V.do(ve.tensor_tensor, U[:, 6 + fc, 0:N], O[:, fc, 0:N], U[:, UG + fc, 0:N], ALU.mult)
            return everyone()

        def finish(wait):
            for e in (T, V, G):
                e.flush()
            outs = semaphore("out_landed")
            A.wait(*wait)
            A.flush()
            ac.dma_start(out, X[:, :, 0:SEQ]).then_inc(outs, 16)
            ac.wait_ge(outs, 16)

        with ExitStack() as first:
            cv = sb("cv", [P, NC, 2], F32, first)
            t = load(A, (cv[:], cvec))
            A.wait(t)
            t_cv = A.do(ac.activation, cv[:], cv[:], ACT.Silu)
            A.wait(t_cv_x, t_const)
            V.wait(t_cv_x, t_const)
            T.wait(t_const)
            with ExitStack() as scope:
                ring = modulation_buffers("start", 8, scope)
                for s in range(8):
                    modulation_fetch(ring, s, s)
                for c in range(NC):
                    squares(X[:, c:c + 1, :], c % 2, True, chunk=c)
                squares_end(True)
                for s in range(0, 8, 2):
                    terms = modulation_terms(ring, s, Ticket(ada_in[s], 16))
                    modulation_direct(ring, s + 1, 0, s + 1, Ticket(ada_in[s + 1], 16))
                    modulation_sum(s, 0, s, terms)
                V.wait(Ticket(V.sem, V.n))
                one_plus(0, SC_A)
                ada_count[0] = 1

            def ada_in_ffn(scope, g):
                if g == 0:
                    ada_ring.append(modulation_buffers("ffn", 2, scope))
                    return modulation_beside(ada_ring[0], 1, 0, 1, 4)
                return modulation_beside(ada_ring[0], 1, 8, 2, 4, False) if g == 1 else None
            ada_ring = []
            split(0)
            for l in range(DEPTH):
                full = l < DEPTH - 1
                if l:
                    V.wait(Ticket(V.sem, V.n))
                    one_plus(l, SC_A)
                    one_plus(l, SC_F, 1)

                def gain_of(j, l=l):
                    return lambda c, q: mod[:, l, j + c, q:q + 1]

                with ExitStack() as mixing:
                    U = sb(f"U_{l}", [P, UN, TOK], F32, mixing)
                    with ExitStack() as scope:
                        XH = sb(f"XHp_{l}", [P, NC, TOK], F32R, scope)
                        XL = sb(f"XLp_{l}", [P, NC, TOK], F32R, scope)
                        free = everyone()
                        if l:
                            squares_end(True)
                        ready = normed(XH, XL, True, gain_of(SC_A), gain_of(SH_A), free)


                        def project(ctx):
                            def epilogue(c, j, t):
                                A.wait(t)
                                ta = A.do(ac.activation, U[:, ds(c, 1), 0:SEQ], PS[:, j:j + 1, 0:SEQ], ACT.Copy)
                                bank[j].set(ta)
                                if ctx:
                                    V.wait(t)
                                    tv = V.do(ve.tensor_copy, U[:, ds(c, 1), SEQ:TOK], PS[:, 2 + j:3 + j, 0:CTX])
                                    bank[2 + j].set(tv)
                            return epilogue
                        if full:
                            ring = modulation_buffers("win", 2, scope)
                            gemm(UN // 2, NC, (XH, XL), ready, True, project(True),
                                 beside=modulation_beside(ring, 0, 8, 2, 4))
                            one_plus(0, SC_F)
                        else:
                            gemm(UK // 2, NC, (XH, XL), ready, False, project(False))
                            gemm((UHQ - UK) // 2, NC, (XH, XL), ready, True, project(True), first=UK // 2)
                            gemm((UN - UHQ) // 2, NC, (XH, XL), ready, False, project(False), first=UHQ // 2)
                    t = fourier(l, U, full, everyone())
                    t = attention1(l, U, full, t)
                    t = hgrn(l, U, full, t)
                    with ExitStack() as scope:
                        N = TOK if full else SEQ
                        XH = sb(f"XHo_{l}", [P, NC, N], F32R, scope)
                        XL = sb(f"XLo_{l}", [P, NC, N], F32R, scope)
                        ready = split_chunks(XH, XL, lambda c: U[:, c, :], NC, full, t, t)
                        add = add_to_x(l, G_A, full, 0, full)
                        squares_begin(full)
                        gemm(NC // 2, NC, (XH, XL), ready, full, lambda c, j, t: add(c, 0, j, t))
                ffn(f"f{l}", full, gain_of(SC_F), gain_of(SH_F),
                    add_to_x(l, G_F, full, len(GROUPS) - 1, full), lambda full=full: squares_begin(full),
                    ada=ada_in_ffn if l == 0 else None)
            squares_end(False)
            V.take(c_RS)
            V.take(c_X)
            for c in range(NC):
                t = V.do(ve.scalar_tensor_tensor, X[:, c, 0:SEQ], X[:, c, 0:SEQ], col("final", c), RS[:, 0:SEQ],
                         ALU.mult, ALU.mult)
                t_sq = squares(X[:, c:c + 1, 0:SEQ], c % 2, False, t, chunk=c)
            c_RS.add(t)
            c_X.set(t, t_sq)

        YS = [sb(f"YS{s}", [P, SEQ]) for s in range(2)]
        c_YS = [Carry(book), Carry(book)]
        for y in c_YS:
            y.set(*everyone())

        def post_norm(src, g, half, ready, more):
            A.wait(*ready)
            V.wait(*ready)
            squares_end(False)
            t = V.do(ve.tensor_scalar, col("post", g * NC, NC), col("post", g * NC, NC), 0.5 if half else 1.0, None,
                     ALU.mult)
            V.wait(t)
            V.take(c_X)
            V.take(c_RS)
            t_sq = None
            t = scaled(0, src, g)
            for c in range(NC):
                t_next = scaled(c + 1, src, g) if c + 1 < NC else None
                V.wait(t)
                t = V.do(ve.tensor_tensor, X[:, c, 0:SEQ], X[:, c, 0:SEQ], YS[c % 2][:], ALU.add)
                c_YS[c % 2].set(t)
                if more:
                    t_sq = squares(X[:, c:c + 1, 0:SEQ], c % 2, False, t, chunk=c)
                t_x, t = t, t_next
            c_RS.add(t_x)
            c_X.set(t_x, t_sq)
            out_ready.append(t_x)

        def scaled(c, src, g):
            V.take(c_YS[c % 2])
            return V.do(ve.scalar_tensor_tensor, YS[c % 2][:], src(c)[:, 0:SEQ], col("post", g * NC + c),
                        RS[:, 0:SEQ], ALU.mult, ALU.mult)

        out_ready = []

        def pre_gain(g):
            return lambda c, q: col("pre", g * NC + c)

        def store(dst, summed=False):
            def epilogue(c, j, t):
                A.wait(t)
                ta = A.do(ac.activation, dst(c), PS[:, j:j + 1, :], ACT.Copy)
                if summed:
                    ta = squares(PS[:, j:j + 1, :], j, False, t)
                bank[j].set(ta)
            return epilogue

        def ffn2(tag, g, final=False):
            with ExitStack() as scope:
                Y = sb(f"Y_{tag}", [P, NC, SEQ], F32, scope)
                c_Y = Carry(book)
                c_Y.set(*everyone())

                def down(c, grp, j, t):
                    V.wait(t)
                    V.take(c_Y)
                    y = Y[:, ds(c, 1), :]
                    if grp == 0:
                        t = V.do(ve.tensor_copy, y, PS[:, j:j + 1, :])
                    else:
                        t = V.do(ve.tensor_tensor, y, PS[:, j:j + 1, :], y, ALU.add)
                    bank[j].set(t)
                    if grp == len(GROUPS) - 1:
                        squares(y, j, False, t)
                    c_Y.set(t)
                ffn(tag, False, pre_gain(g), None, down, lambda: squares_begin(False), final)
                post_norm(lambda c: Y[:, c, :], g, True, c_Y.t, not final)

        def attention2(U, t_in):
            with ExitStack() as scope:
                tab = sb("rope2_t", [P, 2, SEQ], F32, scope)
                cm = sb("cm", [P, P], F32, scope)
                KR = sb("KR2", [P, SEQ], F32, scope)
                KZ = [sb(f"KZ{h}", [P, SEQ], F32, scope) for h in range(2)]
                VT = sb("VT2", [P, SEQ // P, 4 * P], F32, scope)
                for e in (T, A, V, G):
                    e.wait(*t_in)
                t_tab = load(G, (tab[:], rope2), (cm[:], causal))
                V.wait(t_tab)
                cs = (tab[:, 0, :], tab[:, 1, :])
                t_v = token_major(lambda j: VT[:, j // 4, (j % 4) * P:(j % 4 + 1) * P],
                                  lambda j: U[:, 8 + j % 4, (j // 4) * P:(j // 4 + 1) * P], 4 * (SEQ // P), [], [])

                def prep(QR, c):
                    t = rope(KR[:], U[:, ds(c + 4, 1), :].rearrange("p a n -> p (a n)"), SEQ, cs, None, R2, [], [])
                    head_halves([k[:] for k in KZ], KR[:], t, [])
                    return rope(QR[:, 0:SEQ], U[:, ds(c, 1), :].rearrange("p a n -> p (a n)"), SEQ, cs, None, R2,
                                [], [])
                tiles = [(q, 0, q + P, True) for q in range(0, SEQ, P)]
                attend(scope, "m", lambda c, q0: U[:, ds(c, 1), q0:q0 + P], 4, prep, tiles,
                       lambda kv, h, k0, n: KZ[h][:, k0:k0 + n],
                       lambda c, kt: VT[:, kt, ds(c * P, P)], lambda kv, h: h, 1, [t_v], t_tab, cm[:])
            return everyone()

        def lru(U, t_in):
            with ExitStack() as scope:
                WG = sb("WG", [P, 2, 4, P], F32, scope)
                xc = [sb(f"xc{s}", [P, SEQ], F32, scope) for s in range(2)]
                r_, i_, u_, a_ = ([sb(f"lru_{n}{s}", [P, SEQ], F32, scope) for s in range(2)] for n in "riua")
                sp_ = sb("sp_", [P, 4], F32, scope)
                sq_ = sb("sq_", [P, 4], F32, scope)
                for e in (T, A, V, G):
                    e.wait(*t_in)
                t_w = load(G, (WG[:], lru_gates))
                t = A.do(ac.activation, sp_[:], col("lam", 0, 4), ACT.Abs)
                A.wait(t)
                t = A.do(ac.activation, sp_[:], sp_[:], ACT.Exp, scale=-1.0)
                V.wait(t)
                t = V.do(ve.tensor_scalar, sp_[:], sp_[:], 1.0, None, ALU.add)
                A.wait(t)
                t = A.do(ac.activation, sp_[:], sp_[:], ACT.Ln)
                t2 = V.do(ve.tensor_scalar, sq_[:], col("lam", 0, 4), -1.0, 0.0, ALU.mult, ALU.max)
                V.wait(t, t2)
                t = V.do(ve.tensor_tensor, sp_[:], sp_[:], sq_[:], ALU.add)
                V.wait(t)
                t_sp = V.do(ve.tensor_scalar, sp_[:], sp_[:], -8.0, None, ALU.mult)
                c_u = [Carry(book), Carry(book)]
                for c in range(4):
                    s = c % 2
                    V.take(c_u[s])
                    A.take(c_u[s])
                    src, x = U[:, 12 + c, :], xc[s]
                    t = V.do(ve.tensor_scalar, x[:], src, col("conv_w", 3 * 4 + c), col("conv_b", c),
                             ALU.mult, ALU.add)
                    for back in range(1, 4):
                        V.wait(t)
                        t = V.do(ve.scalar_tensor_tensor, x[:, back:SEQ], src[:, 0:SEQ - back],
                                 col("conv_w", (3 - back) * 4 + c), x[:, back:SEQ], ALU.mult, ALU.add)
                    V.wait(t)
                    T.wait(t, t_w)
                    ts = []
                    for g, (dst, b) in enumerate(((r_[s], "ba"), (i_[s], "bx"))):
                        T.take(bank[2 * s + g])
                        t = T.do(te.matmul, PS[:, 2 * s + g, :], WG[:, g, c, :], x[:], start=True, stop=True)
                        A.wait(t)
                        t = A.do(ac.activation, dst[:], PS[:, 2 * s + g, :], ACT.Sigmoid, bias=col(b, c))
                        bank[2 * s + g].set(t)
                        ts.append(t)
                    t_gelu = A.do(ac.activation, U[:, 16 + c, :], U[:, 16 + c, :], ACT.Gelu_apprx_tanh)
                    V.wait(ts[0], t_sp)
                    t = V.do(ve.tensor_scalar, r_[s][:], r_[s][:], sp_[:, c:c + 1], None, ALU.mult)
                    A.wait(t)
                    t_a = A.do(ac.activation, a_[s][:], r_[s][:], ACT.Exp)
                    t_t = A.do(ac.activation, u_[s][:], r_[s][:], ACT.Tanh, scale=-1.0)
                    V.wait(t_a, t_t, ts[1])
                    t1 = V.do(ve.tensor_tensor, r_[s][:], a_[s][:], a_[s][:], ALU.mult)
                    V.wait(t1)
                    t1 = V.do(ve.scalar_tensor_tensor, u_[s][:], r_[s][:], 1.0, u_[s][:], ALU.add, ALU.mult)
                    V.wait(t1)
                    t1 = V.do(ve.tensor_scalar, u_[s][:], u_[s][:], 1e-34, None, ALU.max)
                    t2 = V.do(ve.tensor_tensor, i_[s][:], i_[s][:], x[:], ALU.mult)
                    A.wait(t1)
                    t = A.do(ac.activation, u_[s][:], u_[s][:], ACT.Sqrt)
                    V.wait(t, t2)
                    t = V.do(ve.tensor_tensor, u_[s][:], u_[s][:], i_[s][:], ALU.mult)
                    V.wait(t)
                    t = V.do(ve.tensor_tensor_scan, r_[s][:], a_[s][:], u_[s][:], 0.0, ALU.mult, ALU.add)
                    V.wait(t, t_gelu)
                    t = V.do(ve.tensor_tensor, U[:, 4 + c, :], r_[s][:], U[:, 16 + c, :], ALU.mult)
                    c_u[s].set(t)
            return everyone()

        def short_conv(U, t_in):
            with ExitStack() as scope:
                y = [sb(f"y{s}", [P, SEQ], F32, scope) for s in range(2)]
                c_y = [Carry(book), Carry(book)]
                V.wait(*t_in)
                for c in range(NC):
                    s = c % 2
                    cx = U[:, 16 + c, :]
                    t = V.do(ve.tensor_tensor, cx, cx, U[:, 8 + c, :], ALU.mult)
                    V.wait(t)
                    V.take(c_y[s])
                    t = V.do(ve.tensor_scalar, y[s][:], cx, col("c_conv", 2 * NC + c), None, ALU.mult)
                    for back in range(1, 3):
                        V.wait(t)
                        t = V.do(ve.scalar_tensor_tensor, y[s][:, back:SEQ], cx[:, 0:SEQ - back],
                                 col("c_conv", (2 - back) * NC + c), y[s][:, back:SEQ], ALU.mult, ALU.add)
                    V.wait(t)
                    t = V.do(ve.tensor_tensor, U[:, c, :], U[:, c, :], y[s][:], ALU.mult)
                    c_y[s].set(t)
            return everyone()

        for l in range(DEPTH):
            ffn2(f"a{l}", 3 * l)
            n_in = (20, 24)[l]
            with ExitStack() as mixing:
                U = sb(f"U2_{l}", [P, n_in, SEQ], F32, mixing)
                with ExitStack() as scope:
                    XH = sb(f"XHq_{l}", [P, NC, SEQ], F32R, scope)
                    XL = sb(f"XLq_{l}", [P, NC, SEQ], F32R, scope)
                    free = everyone()
                    squares_end(False)
                    ready = normed(XH, XL, False, pre_gain(3 * l + 1), None, free)
                    gemm(n_in // 2, NC, (XH, XL), ready, False, store(lambda c: U[:, ds(c, 1), :]))
                if l == 0:
                    t = attention2(U, everyone())
                    t = lru(U, t)
                else:
                    t = short_conv(U, everyone())
                with ExitStack() as scope:
                    XH = sb(f"XHr_{l}", [P, NC, SEQ], F32R, scope)
                    XL = sb(f"XLr_{l}", [P, NC, SEQ], F32R, scope)
                    ready = split_chunks(XH, XL, lambda c: U[:, c, :], NC, False, t, t)
                    squares_begin(False)
                    gemm(NC // 2, NC, (XH, XL), ready, False, store(lambda c: U[:, ds(c + 8, 1), :], True))
                    post_norm(lambda c: U[:, 8 + c, :], 3 * l + 1, False, everyone(), True)
            ffn2(f"b{l}", 3 * l + 2, final=l == DEPTH - 1)
        finish(everyone())


def rotation(pairs, heads=2, source=None):
    m = np.zeros((P, P), np.float32)
    for h in range(heads):
        base = (source if source is not None else h) * HD
        for first, w in pairs:
            for j in range(first, first + w):
                m[base + j + w, h * HD + j] = -1
                m[base + j, h * HD + j + w] = 1
    return m


def block_diagonal(a):
    m = np.zeros((P, P), np.float32)
    m[:HD, :HD] = m[HD:, HD:] = a
    return m


def tables():
    f = np.float32
    d = np.arange(HD)
    ang = 2 * np.pi * ((d[:, None] * d[None, :]) % HD) / HD
    axial = [(0, 16), (32, 16)]
    copy = [np.zeros((P, P), f) for _ in range(2)]
    for kv in range(2):
        for h in range(2):
            copy[kv][kv * HD + d, h * HD + d] = 1
    mats = np.stack([
        np.full((P, P), 1 / D, f), np.eye(P, dtype=f), block_diagonal(np.full((HD, HD), 1 / HD, f)),
        rotation(axial), copy[0], copy[1], rotation(axial, source=0), rotation(axial, source=1),
        rotation([(0, 8)]), block_diagonal(np.cos(ang) / 8), block_diagonal(np.sin(ang) / 8),
    ], 1).astype(f)

    def dft(n):
        a = 2 * np.pi * ((np.arange(n)[:, None] * np.arange(n)[None, :]) % n) / n
        t = np.stack([np.cos(a), -np.sin(a)]) / np.sqrt(n)
        return np.ascontiguousarray(t.reshape(2, n // P, P, n).transpose(2, 0, 1, 3)).astype(f)

    freqs = (f(10000.0) ** (-np.arange(0, 32, 2, dtype=f) / f(32))).astype(f)
    pos = np.arange(SEQ)
    ar = ((pos // 64).astype(f)[:, None] * freqs).T
    ak = ((pos % 64).astype(f)[:, None] * freqs).T
    angles = np.concatenate([ar, ar, ak, ak] * 2, 0)
    rope1 = np.zeros((P, 2, TOK), f)
    rope1[:, 0] = 1
    rope1[:, 0, :SEQ], rope1[:, 1, :SEQ] = np.cos(angles), np.sin(angles)
    inv = (f(500000.0) ** (-np.arange(0, 16, 2, dtype=f) / f(16))).astype(f)
    a2 = (pos.astype(f)[:, None] * inv).T
    rope2 = np.zeros((P, 2, SEQ), f)
    rope2[:, 0] = 1
    for h in range(2):
        for part in range(2):
            rope2[h * HD + part * 8:h * HD + part * 8 + 8, 0] = np.cos(a2)
            rope2[h * HD + part * 8:h * HD + part * 8 + 8, 1] = np.sin(a2)
    masks = np.zeros((P, 2, LEVELS, P), f)
    s, t = np.arange(P)[:, None], np.arange(P)[None, :]
    for lv in range(LEVELS):
        h = P >> (lv + 1)
        same = s // (2 * h) == t // (2 * h)
        masks[:, 0, lv] = same & (s % (2 * h) < h) & (t % (2 * h) >= h)
        masks[:, 1, lv] = same & (s % (2 * h) >= h) & (t % (2 * h) < h)
    causal = np.where(np.arange(P)[None, :] <= np.arange(P)[:, None], 0, NEG).astype(f)
    return dict(mats=mats, rope1=rope1, rope2=rope2, dft_x=dft(SEQ), dft_c=dft(CTX), masks=masks, causal=causal,
                head_mask=np.repeat(np.eye(2, dtype=f), HD, 0))


def chunks(v):
    v = np.asarray(v)
    v = v.reshape(v.shape[:-1] + (v.shape[-1] // P, P))
    return np.moveaxis(v, -1, 0).reshape(P, -1)


def column_panels(w):
    k, n = w.shape
    w = w.reshape(k // P, P, n // 256, 256).transpose(2, 1, 0, 3)
    if k < D:
        w = np.concatenate([w, np.zeros((n // 256, P, (D - k) // P, 256), w.dtype)], 2)
    return w.reshape(n // 256, P, PANEL)


def ffn_panels(gate, up, down):
    both = np.concatenate([gate.reshape(D, DFF // P, P), up.reshape(D, DFF // P, P)], 2).reshape(D, 2 * DFF)
    both = column_panels(both)
    out, at = [], 0
    for nk in GROUPS:
        out += [both[at:at + nk], column_panels(down[at * P:(at + nk) * P])]
        at += nk
    return out


def lay_out(a):
    a = {k: np.asarray(v) for k, v in a.items()}
    x = np.concatenate([a["x"][0], a["ctx"][0]], 0)
    xT = np.ascontiguousarray(x.T.reshape(NC, P, TOK).transpose(1, 0, 2))
    cvec = np.ascontiguousarray(np.stack([chunks(a["c"][0]), chunks(a["c_ctx"])], 2))
    two = lambda v: np.concatenate([v, v], -1)
    cols = np.concatenate([
        chunks(a["b_ada"]), two(a["q_norm"]).T, two(a["k_norm"]).T, two(a["hg_norm"]).T, chunks(a["hg_lb_logits"]),
        chunks(a["final_norm"]), chunks(a["norm_pre_2"]), chunks(a["norm_post_2"]), chunks(a["lru_conv_w_2"][0]),
        chunks(a["lru_conv_b_2"][0]), chunks(a["lru_gate_a_b_2"].reshape(-1)),
        chunks(a["lru_gate_x_b_2"].reshape(-1)), chunks(a["lru_lambda_2"][0]), chunks(a["c_conv_w_2"][0]),
    ], 1)
    parts = []
    for l in range(DEPTH):
        parts += [column_panels(a["w_in"][l]), column_panels(a["w_out"][l])]
        parts += ffn_panels(a["w_gate"][l], a["w_up"][l], a["w_down"][l])
    for l in range(DEPTH):
        parts += ffn_panels(a["ffn1_w_gate_2"][l], a["ffn1_w_up_2"][l], a["ffn1_w_down_2"][l])
        w_in, w_out = (a["ab_w_in_2"][0], a["ab_w_out_2"][0]) if l == 0 else (a["c_w_in_2"][0], a["c_w_out_2"][0])
        parts += [column_panels(w_in), column_panels(w_out)]
        parts += ffn_panels(a["ffn2_w_gate_2"][l], a["ffn2_w_up_2"][l], a["ffn2_w_down_2"][l])
    panels = np.concatenate(parts, 0)
    assert len(panels) % 2 == 0, len(panels)
    ada = np.concatenate([column_panels(a["w_ada"][l]) for l in range(DEPTH)], 0)
    w_four = np.ascontiguousarray(a["w_four"].reshape(DEPTH, 2, P, 2 * P).transpose(0, 2, 1, 3))
    gates = np.zeros((P, 2, 4, P), np.float32)
    for g, w in enumerate((a["lru_gate_a_w_2"][0], a["lru_gate_x_w_2"][0])):
        for h in range(8):
            r = slice((h % 2) * HD, (h % 2 + 1) * HD)
            gates[r, g, h // 2, r] = w[h]
    return dict(xT=xT, cvec=cvec, cols=np.ascontiguousarray(cols), panels=panels, ada_panels=ada, w_four=w_four,
                lru_gates=gates, **tables())


def kernel(**inputs):
    import concourse.bacc as bacc
    from concourse.bass_utils import run_bass_kernel_spmd

    arrays = lay_out(inputs)
    nc = bacc.Bacc("TRN2", target_bir_lowering=False, num_devices=1, dynamic_dma_scratch_size=4096)
    args = {n: nc.dram_tensor(f"in_{n}", v.shape, mybir.dt.from_np(v.dtype), kind="ExternalInput").ap()
            for n, v in arrays.items()}
    out = nc.dram_tensor("out_0", (P, NC, SEQ), F32, kind="ExternalOutput").ap()
    program(nc, out=out, **args)
    r = run_bass_kernel_spmd(nc, [{f"in_{n}": v for n, v in arrays.items()}], core_ids=[0])
    got = r.results[0]["out_0"]
    return got.transpose(2, 1, 0).reshape(1, SEQ, D)
```
